# Optimizing a Trainium2 kernel written in Bass

```python
import math
import jax, jax.numpy as jnp
from jax import lax
import numpy as np

D_MODEL = 1024
BATCH = 1
SEQ = 1024
DEPTH = 1

CHUNK = 64
QBLOCK = 128
MIX_WIDTH = D_MODEL
DIFF_HEADS = 4
DIFF_DH = 64
DIFF_VD = 2 * DIFF_DH
FOX_HEADS = 8
FOX_DH = 64
ROPE_THETA = 500000.0
ROPE_DIM = DIFF_DH // 4
D_FF = ((8 * D_MODEL // 3 + 255) // 256) * 256
EPS = 1e-5
NEG = -1e30

DIFF_QK_W = DIFF_HEADS * 2 * DIFF_DH
DIFF_V_W = DIFF_HEADS * DIFF_VD
FOX_W = FOX_HEADS * FOX_DH
PROJ_W = 2 * DIFF_QK_W + DIFF_V_W + 3 * FOX_W + FOX_HEADS
SPLITS = (DIFF_QK_W,
          2 * DIFF_QK_W,
          2 * DIFF_QK_W + DIFF_V_W,
          2 * DIFF_QK_W + DIFF_V_W + FOX_W,
          2 * DIFF_QK_W + DIFF_V_W + 2 * FOX_W,
          2 * DIFF_QK_W + DIFF_V_W + 3 * FOX_W)


def rmsnorm(x, g):
    xf = x.astype(jnp.float32)
    y = xf * lax.rsqrt(jnp.mean(xf * xf, axis=-1, keepdims=True) + EPS)
    return (y * g.astype(jnp.float32)).astype(x.dtype)

def rope_partial(t, cos, sin):
    half = ROPE_DIM // 2
    shp = (1, t.shape[1]) + (1,) * (t.ndim - 3) + (half,)
    c = cos.reshape(shp).astype(t.dtype)
    s = sin.reshape(shp).astype(t.dtype)
    t1 = t[..., :half]
    t2 = t[..., half:ROPE_DIM]
    return jnp.concatenate([t1 * c - t2 * s, t2 * c + t1 * s, t[..., ROPE_DIM:]], axis=-1)

def to_blocks(t, nb):
    b, _, h, d = t.shape
    return t.reshape(b, nb, QBLOCK, h, d).transpose(1, 0, 3, 2, 4)

def from_blocks(t):
    nb, b, h, q, d = t.shape
    return t.transpose(1, 0, 3, 2, 4).reshape(b, nb * q, h * d)

def first_inputs(seed: int = 0) -> dict:
    key = jax.random.key(seed)
    ks = jax.random.split(key, 16)
    f32 = jnp.float32
    nrm = lambda k, shp, s: jax.random.normal(k, shp, f32) * s
    return {
        "x": jax.random.normal(ks[0], (BATCH, SEQ, D_MODEL), f32),
        "norm1_g": 1.0 + nrm(ks[1], (DEPTH, D_MODEL), 0.02),
        "w_in": nrm(ks[2], (DEPTH, D_MODEL, PROJ_W), D_MODEL ** -0.5),
        "b_f": 3.0 + nrm(ks[3], (DEPTH, FOX_HEADS), 0.5),
        "lam_q1": nrm(ks[4], (DEPTH, DIFF_DH), 0.1),
        "lam_k1": nrm(ks[5], (DEPTH, DIFF_DH), 0.1),
        "lam_q2": nrm(ks[6], (DEPTH, DIFF_DH), 0.1),
        "lam_k2": nrm(ks[7], (DEPTH, DIFF_DH), 0.1),
        "subln_g": 1.0 + nrm(ks[8], (DEPTH, DIFF_VD), 0.02),
        "w_out": nrm(ks[9], (DEPTH, MIX_WIDTH, D_MODEL), MIX_WIDTH ** -0.5),
        "norm2_g": 1.0 + nrm(ks[10], (DEPTH, D_MODEL), 0.02),
        "w_gate": nrm(ks[11], (DEPTH, D_MODEL, D_FF), D_MODEL ** -0.5),
        "w_up": nrm(ks[12], (DEPTH, D_MODEL, D_FF), D_MODEL ** -0.5),
        "w_down": nrm(ks[13], (DEPTH, D_FF, D_MODEL), D_FF ** -0.5),
        "normf_g": 1.0 + nrm(ks[14], (D_MODEL,), 0.02),
    }

def first_block(x, norm1_g, w_in, b_f, lam_q1, lam_k1, lam_q2, lam_k2, subln_g, w_out,
              norm2_g, w_gate, w_up, w_down, normf_g):
    f32 = jnp.float32
    B, S, _ = x.shape
    nb = S // QBLOCK
    pos = jnp.arange(S, dtype=jnp.int32)
    inv_freq = ROPE_THETA ** (-jnp.arange(0, ROPE_DIM, 2, dtype=f32) / ROPE_DIM)
    ang = pos.astype(f32)[:, None] * inv_freq[None, :]
    cos, sin = jnp.cos(ang), jnp.sin(ang)
    k_chunk = pos // CHUNK
    scale_d = DIFF_DH ** -0.5
    scale_f = FOX_DH ** -0.5

    for l in range(DEPTH):
        lam_init = 0.8 - 0.6 * math.exp(-0.3 * l)
        h = rmsnorm(x, norm1_g[l])
        proj = jnp.einsum('bsd,de->bse', h, w_in[l])
        dq, dk, dv, fq, fk, fv, fg = jnp.split(proj, SPLITS, axis=-1)

        dq = rope_partial(dq.reshape(B, S, DIFF_HEADS, 2, DIFF_DH), cos, sin)
        dk = rope_partial(dk.reshape(B, S, DIFF_HEADS, 2, DIFF_DH), cos, sin)
        dv_t = dv.reshape(B, S, DIFF_HEADS, DIFF_VD).transpose(0, 2, 1, 3)
        k1 = dk[:, :, :, 0].transpose(0, 2, 1, 3)
        k2 = dk[:, :, :, 1].transpose(0, 2, 1, 3)
        lam = (jnp.exp(jnp.sum(lam_q1[l].astype(f32) * lam_k1[l].astype(f32)))
               - jnp.exp(jnp.sum(lam_q2[l].astype(f32) * lam_k2[l].astype(f32)))
               + lam_init)

        fq = fq.reshape(B, S, FOX_HEADS, FOX_DH)
        fk_t = fk.reshape(B, S, FOX_HEADS, FOX_DH).transpose(0, 2, 1, 3)
        fv_t = fv.reshape(B, S, FOX_HEADS, FOX_DH).transpose(0, 2, 1, 3)
        log_f = jax.nn.log_sigmoid((fg + b_f[l]).astype(f32))
        cum = jnp.cumsum(log_f, axis=1).transpose(0, 2, 1)
        cum_blocks = cum.reshape(B, FOX_HEADS, nb, QBLOCK).transpose(2, 0, 1, 3)

        def block(args):
            i, q1b, q2b, qfb, cqb = args
            qpos = i * QBLOCK + jnp.arange(QBLOCK, dtype=jnp.int32)
            chunk_mask = k_chunk[None, :] <= (qpos // CHUNK)[:, None]
            causal = pos[None, :] <= qpos[:, None]
            s1 = jnp.einsum('bhqd,bhkd->bhqk', q1b, k1, preferred_element_type=f32) * scale_d
            s2 = jnp.einsum('bhqd,bhkd->bhqk', q2b, k2, preferred_element_type=f32) * scale_d
            p = (jax.nn.softmax(jnp.where(chunk_mask, s1, NEG), axis=-1)
                 - lam * jax.nn.softmax(jnp.where(chunk_mask, s2, NEG), axis=-1))
            od = jnp.einsum('bhqk,bhkd->bhqd', p.astype(dv_t.dtype), dv_t)
            sf = (jnp.einsum('bhqd,bhkd->bhqk', qfb, fk_t, preferred_element_type=f32) * scale_f
                  + cqb[:, :, :, None] - cum[:, :, None, :])
            pf = jax.nn.softmax(jnp.where(causal, sf, NEG), axis=-1)
            of = jnp.einsum('bhqk,bhkd->bhqd', pf.astype(fv_t.dtype), fv_t)
            return od, of

        od_b, of_b = lax.map(block, (jnp.arange(nb, dtype=jnp.int32),
                                     to_blocks(dq[:, :, :, 0], nb),
                                     to_blocks(dq[:, :, :, 1], nb),
                                     to_blocks(fq, nb),
                                     cum_blocks))
        od_b = rmsnorm(od_b, subln_g[l]) * (1.0 - lam_init)
        mix = jnp.concatenate([from_blocks(od_b), from_blocks(of_b)], axis=-1)
        x = x + jnp.einsum('bse,ed->bsd', mix, w_out[l])

        h2 = rmsnorm(x, norm2_g[l])
        g = jnp.einsum('bsd,df->bsf', h2, w_gate[l])
        u = jnp.einsum('bsd,df->bsf', h2, w_up[l])
        x = x + jnp.einsum('bsf,fd->bsd', jax.nn.silu(g) * u, w_down[l])

    return rmsnorm(x, normf_g)


MIX_WIDTH_2 = D_MODEL
CONV_A_WIDTH = D_MODEL // 4
CONV_A_K = 3
CONV_B_WIDTH = D_MODEL // 4
CONV_B_K = 31
SB_HEAD_DIM = 64
SB_HEADS = (MIX_WIDTH_2 - CONV_A_WIDTH - CONV_B_WIDTH) // SB_HEAD_DIM
SB_WIDTH = SB_HEADS * SB_HEAD_DIM
SB_BLOCK = 128
D_FF_2 = 4 * D_MODEL
IN_COLS = 3 * CONV_A_WIDTH + 2 * CONV_B_WIDTH + 3 * SB_WIDTH
RMS_EPS = 1e-6
LN_EPS = 1e-5


def _rmsnorm(x, g):
    xf = x.astype(jnp.float32)
    y = xf * lax.rsqrt(jnp.mean(xf * xf, axis=-1, keepdims=True) + RMS_EPS)
    return (y * g.astype(jnp.float32)).astype(x.dtype)

def _layernorm(x, g, b):
    xf = x.astype(jnp.float32)
    mu = jnp.mean(xf, axis=-1, keepdims=True)
    var = jnp.mean(jnp.square(xf - mu), axis=-1, keepdims=True)
    y = (xf - mu) * lax.rsqrt(var + LN_EPS)
    return (y * g.astype(jnp.float32) + b.astype(jnp.float32)).astype(x.dtype)

def _causal_dwconv(x, w):
    k, c = w.shape
    return lax.conv_general_dilated(
        x, w[:, None, :].astype(x.dtype),
        window_strides=(1,), padding=((k - 1, 0),),
        dimension_numbers=("NWC", "WIO", "NWC"),
        feature_group_count=c)

def _stick_breaking(q, k, v):
    t_len = q.shape[2]
    scale = 1.0 / math.sqrt(q.shape[-1])
    outs = []
    for q0 in range(0, t_len, SB_BLOCK):
        kv_len = q0 + SB_BLOCK
        qb = q[:, :, q0:kv_len]
        kb = k[:, :, :kv_len]
        vb = v[:, :, :kv_len]
        z = jnp.einsum("bhqd,bhkd->bhqk", qb, kb).astype(jnp.float32) * scale
        t_idx = q0 + jnp.arange(SB_BLOCK)[:, None]
        s_idx = jnp.arange(kv_len)[None, :]
        mask = s_idx < t_idx
        log_beta = jax.nn.log_sigmoid(z)
        log_1m = jnp.where(mask, log_beta - z, 0.0)
        suffix = lax.cumsum(log_1m, axis=3, reverse=True) - log_1m
        a = jnp.where(mask, jnp.exp(log_beta + suffix), 0.0)
        outs.append(jnp.einsum("bhqk,bhkd->bhqd", a.astype(v.dtype), vb))
    return jnp.concatenate(outs, axis=2)

def _layer(x, g_attn, w_in, w_conv_a, w_conv_b, b_conv_b, ln_b_g, ln_b_b, w_out,
           g_ffn, w_ff1, w_ff2):
    bsz, t_len, _ = x.shape
    h = _rmsnorm(x, g_attn)
    p = h @ w_in
    o0 = 0
    def take(n):
        nonlocal o0
        s = p[..., o0:o0 + n]
        o0 += n
        return s
    a_b = take(CONV_A_WIDTH)
    a_c = take(CONV_A_WIDTH)
    a_h = take(CONV_A_WIDTH)
    b_glu = take(2 * CONV_B_WIDTH)
    q = take(SB_WIDTH)
    k = take(SB_WIDTH)
    v = take(SB_WIDTH)

    y_a = a_b * _causal_dwconv(a_c * a_h, w_conv_a)

    g = b_glu[..., :CONV_B_WIDTH] * jax.nn.sigmoid(b_glu[..., CONV_B_WIDTH:])
    g = _causal_dwconv(g, w_conv_b) + b_conv_b
    y_b = jax.nn.silu(_layernorm(g, ln_b_g, ln_b_b))

    def heads(t):
        return t.reshape(bsz, t_len, SB_HEADS, SB_HEAD_DIM).transpose(0, 2, 1, 3)
    o = _stick_breaking(heads(q), heads(k), heads(v))
    y_c = o.transpose(0, 2, 1, 3).reshape(bsz, t_len, SB_WIDTH)

    x = x + jnp.concatenate([y_a, y_b, y_c], axis=-1) @ w_out

    h2 = _rmsnorm(x, g_ffn)
    x = x + jnp.square(jax.nn.relu(h2 @ w_ff1)) @ w_ff2
    return x

def second_inputs(seed: int = 0) -> dict:
    key = jax.random.key(seed)
    ks = jax.random.split(key, 14)
    f32 = jnp.float32
    def nrm(k, shape, scale):
        return jax.random.normal(k, shape, f32) * scale
    return {
        "x": nrm(ks[0], (BATCH, SEQ, D_MODEL), 1.0),
        "g_attn": 1.0 + nrm(ks[1], (DEPTH, D_MODEL), 0.02),
        "w_in": nrm(ks[2], (DEPTH, D_MODEL, IN_COLS), D_MODEL ** -0.5),
        "w_conv_a": nrm(ks[3], (DEPTH, CONV_A_K, CONV_A_WIDTH), CONV_A_K ** -0.5),
        "w_conv_b": nrm(ks[4], (DEPTH, CONV_B_K, CONV_B_WIDTH), CONV_B_K ** -0.5),
        "b_conv_b": nrm(ks[5], (DEPTH, CONV_B_WIDTH), 0.02),
        "ln_b_g": 1.0 + nrm(ks[6], (DEPTH, CONV_B_WIDTH), 0.02),
        "ln_b_b": nrm(ks[7], (DEPTH, CONV_B_WIDTH), 0.02),
        "w_out": nrm(ks[8], (DEPTH, MIX_WIDTH_2, D_MODEL), MIX_WIDTH_2 ** -0.5),
        "g_ffn": 1.0 + nrm(ks[9], (DEPTH, D_MODEL), 0.02),
        "w_ff1": nrm(ks[10], (DEPTH, D_MODEL, D_FF_2), D_MODEL ** -0.5),
        "w_ff2": nrm(ks[11], (DEPTH, D_FF_2, D_MODEL), D_FF_2 ** -0.5),
        "g_final": 1.0 + nrm(ks[12], (D_MODEL,), 0.02),
    }

def second_block(x, g_attn, w_in, w_conv_a, w_conv_b, b_conv_b, ln_b_g, ln_b_b, w_out,
              g_ffn, w_ff1, w_ff2, g_final):
    for l in range(DEPTH):
        x = _layer(x, g_attn[l], w_in[l], w_conv_a[l], w_conv_b[l], b_conv_b[l],
                   ln_b_g[l], ln_b_b[l], w_out[l], g_ffn[l], w_ff1[l], w_ff2[l])
    return _rmsnorm(x, g_final)


def setup_inputs(seed=0):
    out = dict(first_inputs(seed))
    for name, value in second_inputs(seed + 1).items():
        if name != "x":
            out[name + "_2"] = value
    return out


def reference(
    x, norm1_g, w_in, b_f, lam_q1, lam_k1, lam_q2, lam_k2, subln_g, w_out, norm2_g, w_gate,
    w_up, w_down, normf_g, g_attn_2, w_in_2, w_conv_a_2, w_conv_b_2, b_conv_b_2, ln_b_g_2,
    ln_b_b_2, w_out_2, g_ffn_2, w_ff1_2, w_ff2_2, g_final_2,
):
    x = first_block(
        x, norm1_g, w_in, b_f, lam_q1, lam_k1, lam_q2, lam_k2, subln_g, w_out, norm2_g, w_gate,
        w_up, w_down, normf_g,
    )
    return second_block(
        x, g_attn_2, w_in_2, w_conv_a_2, w_conv_b_2, b_conv_b_2, ln_b_g_2, ln_b_b_2, w_out_2,
        g_ffn_2, w_ff1_2, w_ff2_2, g_final_2,
    )


_drawn_inputs = setup_inputs


def setup_inputs(seed=0):
    import zlib

    import numpy as np

    out = dict(_drawn_inputs(seed))
    spreads = {}
    factors = {'lam_q2': 2.773,
     'subln_g': 3.939,
     'norm2_g': 3.525,
     'g_attn_2': 3.025,
     'b_conv_b_2': 22.937,
     'ln_b_g_2': 64.0,
     'ln_b_b_2': 64.0,
     'g_ffn_2': 11.287,
     'g_final_2': 8.032}
    for name, (base, spread) in spreads.items():
        noise = np.random.default_rng([zlib.crc32(name.encode()), seed]).standard_normal(out[name].shape)
        drawn = base * np.exp(spread * noise) if base else spread * noise
        out[name] = __import__('jax').numpy.asarray(drawn.astype(out[name].dtype))
    for name, factor in factors.items():
        out[name] = (out[name] * factor).astype(out[name].dtype)
    return out
```

```python
import math

import numpy as np

import concourse.bass as bass
from concourse import mybir

F = mybir.dt.float32
R = mybir.dt.float32r
BF = mybir.dt.bfloat16
ALU = mybir.AluOpType
ACT = mybir.ActivationFunctionType
AX = mybir.AxisListType.X

S = 1024
EPS1 = 1e-5
EPS2 = 1e-6
LN_EPS = 1e-5
LAM_INIT = 0.8 - 0.6 * math.exp(-0.0)

V_G1, V_G2, V_GF, V_GA, V_GFF, V_GFIN = 0, 8, 16, 24, 32, 40
V_SUB, V_BF, V_SGN = 48, 49, 50
V_CA, V_CB, V_BCB, V_LNG, V_LNB, V_LAM = 51, 57, 119, 121, 123, 125
NV = 129
C_ID, C_PERM, C_COS, C_SIN, C_SEL, C_MASK = 0, 128, 256, 1280, 2304, 3328
NC = C_MASK + 3 * 512
DIFF, FOX, STICK = 0, 1, 2


class Token:

    def __init__(self, sem, value=None):
        self.sem, self.value, self.needed = sem, value, False


class Queue:

    def __init__(self, sem):
        self.sem, self.items = sem, []

    def wait(self, *tokens):
        for t in tokens:
            if t is not None:
                t.needed = True
                self.items.append((None, t))

    def do(self, fn):
        t = Token(self.sem)
        self.items.append((fn, t))
        return t

    def after(self):
        self.wait([t for f, t in self.items if f is not None][-1])
        return self

    def matmul(self, *a, **k):
        return self.do(lambda e: e.matmul(*a, **k))

    def transpose(self, *a, **k):
        return self.do(lambda e: e.transpose(*a, **k))

    def activation(self, *a, **k):
        return self.do(lambda e: e.activation(*a, **k))

    def tensor_tensor(self, *a, **k):
        return self.do(lambda e: e.tensor_tensor(*a, **k))

    def tensor_scalar(self, *a, **k):
        return self.do(lambda e: e.tensor_scalar(*a, **k))

    def scalar_tensor_tensor(self, *a, **k):
        return self.do(lambda e: e.scalar_tensor_tensor(*a, **k))

    def tensor_tensor_scan(self, *a, **k):
        return self.do(lambda e: e.tensor_tensor_scan(*a, **k))

    def tensor_copy(self, *a, **k):
        return self.do(lambda e: e.tensor_copy(*a, **k))

    def reduce_max(self, *a, **k):
        return self.do(lambda e: e.reduce_max(*a, **k))

    def reciprocal(self, *a, **k):
        return self.do(lambda e: e.reciprocal(*a, **k))

    def memset(self, *a, **k):
        return self.do(lambda e: e.memset(*a, **k))

    def count(self):
        n = 0
        for fn, t in self.items:
            if fn is not None and t.needed and t.value is None:
                n += 1
                t.value = n

    def emit(self, eng):
        seen = {}
        for fn, t in self.items:
            if fn is None:
                key = id(t.sem)
                if seen.get(key, 0) < t.value:
                    eng.wait_ge(t.sem, t.value)
                    seen[key] = t.value
            else:
                ins = fn(eng)
                if t.needed and t.sem is self.sem:
                    ins.then_inc(t.sem, 1)


def program(nc, args, out, ctx):
    sem = lambda name: ctx.enter_context(nc.semaphore(name))
    PE, DV, AC, SP = (Queue(sem(n)) for n in ("s_pe", "s_dve", "s_act", "s_sp"))

    base = 16512
    place = {}

    def at(name, shape, dt, offset):
        return nc.alloc_sbuf_tensor_at(name, shape, dt, offset=offset)

    def new(name, shape, dt, size):
        nonlocal base
        off = base
        n = 1
        for d in shape[1:]:
            n *= d
        assert n * (2 if dt == BF else 4) <= size
        base += (size + 31) // 32 * 32
        place[name] = off
        return at(name, shape, dt, off)

    RG = [new(f"R{i}", [128, 2, 8, S], R, 65536) for i in range(2)]
    XF = new("X", [128, 8, S], F, 32768)
    x0 = place["X"]
    Pb = at("Pb", [128, 2, 2, S], F, x0)
    PT = at("PT", [128, 2, 2, 512], R, x0 + 16384)
    TABF = at("TABF", [128, 2, S], F, x0 + 24576)
    TABR = at("TABR", [128, 2, S], R, x0 + 24576)
    raw = new("raw", [128, 3, 512], F, 6144)
    wh = new("wh", [128, 4, 512], R, 8192)
    wl = new("wl", [128, 4, 512], R, 8192)
    rstd = new("rstd", [128, S], F, 4096)
    P2 = new("P2", [128, 1032], F, 4128)
    mix = new("mix", [128, S], F, 4096)
    stage = new("stage", [128, 4, 512], F, 8192)
    ident = new("ident", [128, 128], F, 512)
    identb = new("identb", [128, 128], BF, 256)
    ones = new("ones", [128, 128], F, 512)
    perm = new("perm", [128, 128], F, 512)
    maskb = new("maskb", [128, 2, 256], BF, 1024)
    vec = new("vec", [128, NV + 3], F, (NV + 3) * 4)
    cq = new("cq", [128, 64], F, 256)
    sm = new("sm", [128, 32], F, 128)
    assert base <= 229368
    PS = ctx.enter_context(nc.psum_tensor("PS", [128, 8, 512], F))

    scr_mix = nc.dram_tensor("scr_mix", (8, 128, S), F, kind="Internal").ap()
    scr_x = nc.dram_tensor("scr_x", (8, 128, S), F, kind="Internal").ap()
    scr_ct = nc.dram_tensor("scr_ct", (128, S), F, kind="Internal").ap()

    v = lambda i: vec[:, i:i + 1]

    dma_sems = {}

    def dma(slot, dst, src, waits=(), q=None):
        q = q or SP
        if slot not in dma_sems:
            dma_sems[slot] = [sem("d_" + slot), 0, None]
        rec = dma_sems[slot]
        q.wait(*waits)
        if rec[2] is not None:
            q.wait(rec[2])
        rec[1] += 16
        t = Token(rec[0], rec[1])
        rec[2] = t
        q.do(lambda e, s=rec[0]: e.dma_start(dst, src).then_inc(s, 16))
        return t

    bank_free = [[] for _ in range(8)]

    def claim(b):
        PE.wait(*bank_free[b])
        bank_free[b] = []

    dense_banks = [0, 1, 2, 3, 4, 5, 6, 7]
    dense_at = [0]

    def next_bank():
        b = dense_banks[dense_at[0] % len(dense_banks)]
        dense_at[0] += 1
        claim(b)
        return b

    stage_free = [[] for _ in range(4)]
    stage_at = [0]

    def next_stage(q):
        i = stage_at[0] % 4
        stage_at[0] += 1
        q.wait(*stage_free[i])
        stage_free[i] = []
        return i, stage[:, i, :]

    t_vec = dma("vec", vec[:, 0:NV], args["vecs"])
    cst = args["cst"]
    t_id = dma("c0", ident[:, :], cst[:, C_ID:C_ID + 128])
    t_pm = dma("c1", perm[:, :], cst[:, C_PERM:C_PERM + 128])
    DV.wait(t_id)
    t_idb = DV.tensor_copy(identb[:, :], ident[:, :])
    t_ones = DV.memset(ones[:, :], 1.0)

    def load_mask(kind, waits):
        i, st = next_stage(SP)
        t = dma(f"st{i}", st, cst[:, C_MASK + 512 * kind:C_MASK + 512 * kind + 512])
        DV.wait(t, *waits)
        t = DV.tensor_copy(maskb[:, :, :].rearrange("p a b -> p (a b)"), st)
        stage_free[i] = [t]
        return t

    plan = []
    pieces = []
    raw_free = [None] * 3
    hl_free = [None] * 4
    n_load = [0]
    n_split = [0]

    def plan_tile(name, e, k0, nk):
        for k in range(k0, k0 + nk, 4):
            plan.append((name, e, k, min(4, k0 + nk - k)))

    def load_piece():
        n = n_load[0]
        if n >= len(plan) or n >= n_split[0] + 3:
            return
        n_load[0] += 1
        name, e, k, m = plan[n]
        slot = n % 3
        t = dma(f"raw{slot}", raw[:, slot, 0:m * 128].rearrange("p (k c) -> p k c", c=128),
                args[name][e, :, k:k + m, :], waits=[raw_free[slot]])
        pieces.append([t, None, None])

    def split_piece():
        n = n_split[0]
        if n >= len(plan):
            return
        while n_load[0] <= n:
            load_piece()
        n_split[0] += 1
        m = plan[n][3] * 128
        slot, h = n % 3, n % 4
        AC.wait(pieces[n][0], hl_free[h])
        th = AC.activation(wh[:, h, 0:m], raw[:, slot, 0:m], ACT.Copy)
        DV.wait(th)
        tl = DV.tensor_tensor(wl[:, h, 0:m], raw[:, slot, 0:m], wh[:, h, 0:m].bitcast(F), ALU.subtract)
        raw_free[slot] = tl
        pieces[n][1], pieces[n][2] = th, tl
        while n_load[0] < min(len(plan), n_split[0] + 3):
            load_piece()

    used = [0]

    def dense(name, e, k0, nk, src, evac, src_ready=None, s0=0):
        n_p = (nk + 3) // 4
        first = used[0]
        assert plan[first][:3] == (name, e, k0), (plan[first], name, e, k0)
        used[0] += n_p
        for half in range(2):
            b = next_bank()
            cols = slice(512 * half, 512 * half + 512)
            last = None
            for k in range(nk):
                if half == 0 and k % 4 == 0:
                    while n_split[0] < first + k // 4 + 1:
                        split_piece()
                    PE.wait(pieces[first + k // 4][2])
                if src_ready is not None:
                    PE.wait(*src_ready[k])
                h = (first + k // 4) % 4
                kc = slice((k % 4) * 128, (k % 4) * 128 + 128)
                sh, sl = src[:, 0, s0 + k, cols], src[:, 1, s0 + k, cols]
                PE.matmul(PS[:, b, :], wh[:, h, kc], sh, start=(k == 0), stop=False)
                PE.matmul(PS[:, b, :], wh[:, h, kc], sl, start=False, stop=False)
                last = PE.matmul(PS[:, b, :], wl[:, h, kc], sh, start=False, stop=(k == nk - 1))
                if half == 1 and (k % 4 == 3 or k == nk - 1):
                    hl_free[(first + k // 4) % 4] = last
                    if n_split[0] < min(len(plan), used[0] + 2 if k == nk - 1 else used[0] + 1):
                        split_piece()
                elif half == 0 and k == nk - 1 and n_split[0] < used[0] + 1:
                    split_piece()
                if k < nk - 1:
                    yield
            evac(half, b, last)
            yield

    def run(gen):
        for _ in gen:
            pass

    def rsqrt_of(acc, half, dim, eps, dst, waits, extra=None):
        cols = slice(512 * half, 512 * half + 512)
        b = next_bank()
        PE.wait(t_ones, *waits)
        tp = PE.matmul(PS[:, b, :], ones[:, :], acc[:, cols], start=True, stop=True)
        i, va = next_stage(DV)
        j, y = next_stage(AC)
        l, w = next_stage(AC)
        DV.wait(tp)
        if extra is None:
            t = DV.tensor_scalar(va, PS[:, b, :], 1.0 / dim, eps, ALU.mult, ALU.add)
            bank_free[b] = [t]
        else:
            t = extra(va, PS[:, b, :], cols)
            bank_free[b] = [t]
            t = DV.after().tensor_scalar(va, va, 1.0 / dim, eps, ALU.mult, ALU.add)
        AC.wait(t)
        AC.activation(y, va, ACT.Ln)
        ty = AC.after().activation(y, y, ACT.Exp, scale=-0.5)
        tw = AC.after().activation(w, y, ACT.Square)
        DV.wait(tw)
        DV.scalar_tensor_tensor(w, w, -0.5, va, ALU.mult, ALU.mult)
        t = DV.after().scalar_tensor_tensor(dst[:, cols], w, 1.5, y, ALU.add, ALU.mult)
        stage_free[i] = [t]
        stage_free[j] = [t]
        stage_free[l] = [t]
        return t

    hsrc = RG[0]
    ready = [[] for _ in range(8)]
    acc = mix
    for e in range(8):
        tx = dma(f"x{e}", XF[:, e, :], args["xT"][e])
        if e == 0:
            AC.wait(tx)
            t_sq = AC.activation(acc[:, :], XF[:, 0, :], ACT.Square)
            t_acc = t_sq
        else:
            AC.wait(tx, t_acc)
            t_sq = AC.activation(P2[:, 0:S], XF[:, e, :], ACT.Square)
        AC.wait(t_vec)
        th = AC.activation(hsrc[:, 0, e, :], XF[:, e, :], ACT.Copy, scale=v(V_G1 + e))
        if e:
            DV.wait(t_sq)
            t_acc = DV.tensor_tensor(acc[:, :], acc[:, :], P2[:, 0:S], ALU.add)
        DV.wait(th)
        tl = DV.scalar_tensor_tensor(hsrc[:, 1, e, :], XF[:, e, :], v(V_G1 + e), hsrc[:, 0, e, :].bitcast(F), ALU.mult, ALU.subtract)
        ready[e] = [th, tl]
    x_dead = tl
    t_r = [rsqrt_of(acc, h, S, EPS1, rstd, [t_acc]) for h in range(2)]
    rstd_ready = list(t_r)

    lamc = sm[:, 0:1]
    DV.wait(t_vec)
    DV.tensor_tensor(sm[:, 2:4], vec[:, V_LAM:V_LAM + 2], vec[:, V_LAM + 2:V_LAM + 4], ALU.mult)
    g08 = DV.tensor_scalar(sm[:, 1:2], v(V_SUB), 1.0 - LAM_INIT, None, ALU.mult)
    b = next_bank()
    PE.wait(g08)
    t = PE.matmul(PS[:, b, 0:2], ones[:, :], sm[:, 2:4], start=True, stop=True)
    AC.wait(t)
    t = AC.activation(sm[:, 4:6], PS[:, b, 0:2], ACT.Exp)
    bank_free[b] = [t]
    DV.wait(t)
    DV.tensor_tensor(sm[:, 6:7], sm[:, 5:6], sm[:, 4:5], ALU.subtract)
    t_lam = DV.after().tensor_scalar(lamc, sm[:, 6:7], -LAM_INIT, None, ALU.add)

    plan_tile("w_fg", 0, 0, 8)
    for u in range(4):
        for c in (u, 4 + u, 8 + u):
            plan_tile("w_in", c, 0, 8)
    for u in range(4):
        for c in (12 + u, 16 + u, 20 + u):
            plan_tile("w_in", c, 0, 8)
    for e in range(8):
        plan_tile("w_out", e, 0, 8)

    def ffn_plan(groups, up, down):
        t = 0
        for n in groups:
            for i in range(t, t + n):
                for w in up:
                    plan_tile(w, i, 0, 8)
            for e in range(8):
                plan_tile(down, e, t, n)
            t += n

    ffn_plan([8, 7, 7], ["w_gate", "w_up"], "w_down")
    CONV_TILES = [6, 8, 7, 9, 2, 4, 0, 3, 5, 1]
    for c in CONV_TILES:
        plan_tile("w_in2", c, 0, 8)
    for u in range(4):
        for c in (10 + u, 14 + u, 18 + u):
            plan_tile("w_in2", c, 0, 8)
    for e in range(8):
        plan_tile("w_out2", e, 0, 8)
    ffn_plan([8, 8, 8, 8], ["w_ff1"], "w_ff2")

    A_ = [Pb[:, i // 2, i % 2, :] for i in range(4)]

    def fg_evac(half, b, t):
        cols = slice(512 * half, 512 * half + 512)
        DV.wait(t, x_dead, *rstd_ready)
        bank_free[b] = [DV.tensor_tensor(A_[0][:, cols], PS[:, b, :], rstd[:, cols], ALU.mult)]

    run(dense("w_fg", 0, 0, 8, hsrc, fg_evac, ready))
    AC.wait(*bank_free[(dense_at[0] - 1) % 8])
    AC.activation(A_[1], A_[0], ACT.Abs, bias=v(V_BF))
    AC.after().activation(A_[1], A_[1], ACT.Exp, scale=-1.0)
    t = AC.after().activation(A_[1], A_[1], ACT.Ln, bias=1.0)
    DV.after().tensor_scalar(A_[2], A_[0], v(V_BF), 0.0, ALU.add, ALU.min)
    DV.wait(t)
    DV.after().tensor_tensor(A_[2], A_[2], A_[1], ALU.subtract)
    DV.memset(A_[0], 1.0)
    t_cum = DV.after().tensor_tensor_scan(A_[3], A_[0], A_[2], 0.0, ALU.mult, ALU.add)
    DV.after().tensor_scalar(A_[1], A_[3], v(V_SGN), None, ALU.mult)
    ctv = PT[:, 0, :, :].rearrange("p a b -> p (a b)")
    t = DV.after().tensor_copy(ctv, A_[1])
    t = DV.after().tensor_tensor(ctv[32:64, :], A_[1][32:64, :], ctv[32:64, :].bitcast(F), ALU.subtract)
    t_ct = dma("ct", scr_ct, ctv.bitcast(F), waits=[t])
    for half in range(2):
        b = next_bank()
        PE.wait(t_cum, t_id)
        for i in range(4):
            t = PE.transpose(
                PS[:, b, 128 * i:128 * i + 128], A_[3][:, 512 * half + 128 * i:512 * half + 128 * i + 128], ident[:, :])
        DV.wait(t)
        t = DV.tensor_copy(
            cq[:, 32 * half:32 * half + 32].rearrange("p (t h) -> p t h", h=8),
            PS[:, b, :].rearrange("p (t c) -> p t c", c=128)[:, :, 0:8])
        bank_free[b] = [t]
    t_cq = t
    t_tab = dma("tab", TABF[:, :, :].rearrange("p a b -> p (a b)"), cst[:, C_COS:C_COS + 2 * S], waits=[x_dead])
    t_mask = load_mask(DIFF, [])

    class Unit:
        def __init__(self, kind, index, region, half):
            self.kind, self.index = kind, index
            r = region[:, :, :, :].rearrange("p a b s -> p (a b s)")[:, 8192 * half:8192 * half + 8192]
            part = lambda i: r[:, 2048 * i:2048 * i + 2048].rearrange("p (a s) -> p a s", a=2)
            self.QQ, self.KH, self.KL = part(0), part(1), part(2)
            self.V = r[:, 6144:8192].rearrange("p (t c) -> p t c", c=256)
            self.q, self.k, self.v = [], [], []
            self.qk_done = self.pv_done = None

    A0, B0 = slice(0, 64), slice(64, 128)

    def project(u, name, cols, src, prev, freed):
        for which in range(3):
            store = []

            def evac(half, b, t, which=which, store=store):
                cc = slice(512 * half, 512 * half + 512)
                i, st = next_stage(DV)
                DV.wait(t, *rstd_ready)
                td = DV.tensor_tensor(st, PS[:, b, :], rstd[:, cc], ALU.mult)
                bank_free[b] = [td]
                if u.kind == DIFF and which < 2:
                    b2 = next_bank()
                    PE.wait(td, t_pm)
                    tp = PE.matmul(PS[:, b2, :], perm[:, :], st, start=True, stop=True)
                    j, s2 = next_stage(DV)
                    DV.wait(t_tab, tp)
                    tq = DV.tensor_tensor(s2, PS[:, b2, :], TABF[:, 1, cc], ALU.mult)
                    bank_free[b2] = [tq]
                    DV.tensor_tensor(st, st, TABF[:, 0, cc], ALU.mult)
                    td = DV.after().tensor_tensor(st, st, s2, ALU.add)
                    stage_free[j] = [td]
                    u.rope_done = td
                if which < 2:
                    hi, lo = (u.QQ, u.QQ) if which == 0 else (u.KH, u.KL)
                    AC.wait(td, *freed)
                    DV.wait(*freed)
                    if prev is not None:
                        AC.wait(prev.qk_done)
                        DV.wait(prev.qk_done)
                    AC.activation(hi[A0, 0, cc], st[A0, :], ACT.Copy)
                    ta = AC.activation(hi[B0, 1, cc], st[B0, :], ACT.Copy)
                    DV.wait(ta)
                    if which == 0:
                        DV.tensor_tensor(lo[B0, 0, cc], st[A0, :], hi[A0, 0, cc].bitcast(F), ALU.subtract)
                        tl = DV.tensor_tensor(lo[A0, 1, cc], st[B0, :], hi[B0, 1, cc].bitcast(F), ALU.subtract)
                        u.q += [ta, tl]
                    else:
                        DV.tensor_tensor(lo[A0, 0, cc], st[A0, :], hi[A0, 0, cc].bitcast(F), ALU.subtract)
                        tl = DV.tensor_tensor(lo[B0, 1, cc], st[B0, :], hi[B0, 1, cc].bitcast(F), ALU.subtract)
                        u.k += [dma(f"kh0{half}", u.KH[B0, 0, cc].bitcast(F), u.KH[A0, 0, cc].bitcast(F), waits=[ta]),
                                dma(f"kh1{half}", u.KH[A0, 1, cc].bitcast(F), u.KH[B0, 1, cc].bitcast(F), waits=[ta]),
                                dma(f"kl0{half}", u.KL[B0, 0, cc].bitcast(F), u.KL[A0, 0, cc].bitcast(F), waits=[tl]),
                                dma(f"kl1{half}", u.KL[A0, 1, cc].bitcast(F), u.KL[B0, 1, cc].bitcast(F), waits=[tl]), ta, tl]
                    stage_free[i] = [ta, tl]
                else:
                    b2 = next_bank()
                    PE.wait(td, t_id)
                    for n in range(4):
                        tp = PE.transpose(PS[:, b2, 128 * n:128 * n + 128], st[:, 128 * n:128 * n + 128], ident[:, :])
                    stage_free[i] = [tp]
                    tt = slice(4 * half, 4 * half + 4)
                    AC.wait(tp, *freed)
                    if prev is not None:
                        AC.wait(prev.pv_done)
                    if u.kind == DIFF:
                        hi, lo = u.V[:, tt, 0:128], u.V[:, tt, 128:256]
                        ps = PS[:, b2, :].rearrange("p (t c) -> p t c", c=128)
                    else:
                        vv = u.V[:, tt, :].rearrange("p t (a x c) -> p t a x c", a=2, x=2)
                        hi, lo = vv[:, :, :, 0, :], vv[:, :, :, 1, :]
                        ps = PS[:, b2, :].rearrange("p (t a c) -> p t a c", a=2, c=64)
                    ta = AC.activation(hi, ps, ACT.Copy)
                    DV.wait(ta)
                    tl = DV.tensor_tensor(lo, ps, hi.bitcast(F), ALU.subtract)
                    bank_free[b2] = [ta, tl]
                    u.v += [ta, tl]

            yield from dense(name, cols[which], 0, 8, src, evac)

    class Attention:
        SB, TB, OB = [0, 2], 4, 5

        def __init__(self, freed, mask, bias):
            self.job = 0
            self.group = 0
            self.steps = []
            self.p_free = [list(freed), list(freed)]
            self.pt_free = [list(freed), list(freed)]
            self.pt_at = 0
            self.tail = None
            self.mix_free = list(freed)
            self.p2_free = list(freed)
            self.b_free = list(freed)
            self.freed = freed
            self.mask, self.bias = mask, bias
            self.spills = {}

        def scores(self, u, a, i):
            c, par = i // 2, i % 2
            n = 256 * (c + 1)
            s = self.SB[self.job % 2]
            claim(s)
            claim(s + 1)
            PE.wait(*u.q, *u.k, *self.mask)
            q = u.QQ[:, a, 128 * i:128 * i + 128]
            S2 = PS[:, s:s + 2, :].rearrange("p a b -> p (a b)")
            for k0 in range(0, n, 512):
                k1 = min(n, k0 + 512)
                PE.matmul(S2[:, k0:k1], q, u.KH[:, a, k0:k1], start=True, stop=False)
                if u.kind == FOX:
                    h = 2 * u.index + a
                    PE.wait(*self.bias)
                    PE.matmul(S2[:, k0:k1], TABR[:, 1, 128 * h:128 * h + 128], TABR[:, 0, k0:k1], start=False, stop=False)
                if k1 == n:
                    PE.matmul(S2[:, n - 256:n], identb[:, :], maskb[:, par, :], start=False, stop=False)
                t = PE.matmul(S2[:, k0:k1], q, u.KL[:, a, k0:k1], start=False, stop=True)
            u.qk_done = t
            job = dict(u=u, a=a, i=i, n=n, s=s, S2=S2, t=t, slot=self.group % 2, no=self.job)
            self.job += 1
            return job

        def soft1(self, j):
            n, u, S2 = j["n"], j["u"], j["S2"]
            par = j["i"] % 2
            o = 8 + 8 * (j["no"] % 2)
            dst = Pb[:, j["slot"], par, 0:n]
            if u.kind == STICK:
                AC.wait(j["t"], *self.p_free[j["slot"]])
                AC.activation(dst, S2[:, 0:n], ACT.Sigmoid, scale=0.125)
                bt = TABF[:, j["no"] % 2, 0:n]
                if j["no"] >= 2:
                    AC.wait(self.b_used[j["no"] % 2])
                t = AC.activation(bt, S2[:, 0:n], ACT.Sigmoid, scale=-0.125)
                bank_free[j["s"]] = [t]
                bank_free[j["s"] + 1] = [t]
                j["e"] = t
                return
            DV.wait(j["t"])
            tm = DV.reduce_max(sm[:, o:o + 1], S2[:, 0:n], AX)
            if u.kind == DIFF:
                t = DV.after().tensor_scalar(sm[:, o + 1:o + 2], sm[:, o:o + 1], -0.125, None, ALU.mult)
            else:
                h = 2 * u.index + j["a"]
                cqh = cq[:, 8 * j["i"] + h:8 * j["i"] + h + 1]
                DV.wait(t_cq)
                DV.after().scalar_tensor_tensor(sm[:, o + 2:o + 3], sm[:, o:o + 1], 0.125, cqh, ALU.mult, ALU.add)
                t = DV.after().tensor_tensor(sm[:, o + 1:o + 2], cqh, sm[:, o + 2:o + 3], ALU.subtract)
            second = u.kind == DIFF and j["a"] == 1
            if second:
                dst = P2[:, 0:n]
                AC.wait(*self.p2_free)
            else:
                AC.wait(*self.p_free[j["slot"]])
            AC.wait(t, tm)
            t = AC.activation(dst, S2[:, 0:n], ACT.Exp, bias=sm[:, o + 1:o + 2], scale=0.125, accum_out=sm[:, o + 3:o + 4])
            bank_free[j["s"]] = [t]
            bank_free[j["s"] + 1] = [t]
            j["e"] = t

        b_used = [None, None]
        w_read = None

        def soft2(self, j):
            n, u = j["n"], j["u"]
            par = j["i"] % 2
            o = 8 + 8 * (j["no"] % 2)
            dst = Pb[:, j["slot"], par, 0:n]
            DV.wait(j["e"])
            if u.kind == STICK:
                bt = TABF[:, j["no"] % 2, 0:n]
                w = P2[:, S - n:S]
                DV.wait(self.w_read)
                self.b_used[j["no"] % 2] = DV.tensor_tensor_scan(
                    w[:, ::-1], bt[:, ::-1], zeros_for(n), 1.0, ALU.mult, ALU.add)
                j["p"] = DV.after().tensor_tensor(dst, dst, P2[:, S - n + 1:S + 1], ALU.mult)
                self.w_read = j["p"]
                return
            DV.reciprocal(sm[:, o + 4:o + 5], sm[:, o + 3:o + 4])
            if u.kind == DIFF and j["a"] == 1:
                DV.wait(t_lam)
                DV.after().tensor_scalar(sm[:, o + 5:o + 6], sm[:, o + 4:o + 5], lamc, None, ALU.mult)
                t = DV.after().scalar_tensor_tensor(dst, P2[:, 0:n], sm[:, o + 5:o + 6], dst, ALU.mult, ALU.add)
                self.p2_free = [t]
            else:
                t = DV.after().tensor_scalar(dst, dst, sm[:, o + 4:o + 5], None, ALU.mult)
            j["p"] = t

        def group_steps(self, u, a, c, jobs, slot):
            pending = None
            o_first = [True]

            def pv(kp, ps):
                if o_first[0]:
                    claim(self.OB)
                    PE.wait(*u.v)
                for kk in range(2):
                    kt = 2 * kp + kk
                    cc = slice(256 * kk, 256 * kk + 256)
                    if u.kind == DIFF:
                        terms = [(u.V[:, kt, 0:128], 0), (u.V[:, kt, 128:256], 0), (u.V[:, kt, 0:128], 1)]
                    else:
                        vt = u.V[:, kt, 128 * a:128 * a + 128]
                        terms = [(vt, 0), (vt, 1)]
                    for n, (lhs, x) in enumerate(terms):
                        st = o_first[0]
                        o_first[0] = False
                        fin = kt == 2 * c + 1 and n == len(terms) - 1
                        PE.wait(ps[1 + x])
                        t = PE.matmul(
                            PS[:, self.OB, 0:256], lhs, PT[:, ps[0], x, cc], start=st, stop=fin)
                self.pt_free[ps[0]] = [t]
                u.pv_done = t
                return t

            for kp in range(c + 1):
                claim(self.TB)
                PE.wait(jobs[0]["p"], jobs[-1]["p"], *[x["p"] for x in jobs])
                for kk in range(2):
                    for par in range(2):
                        kt = 2 * kp + kk
                        t = PE.transpose(
                            PS[:, self.TB, 256 * kk + 128 * par:256 * kk + 128 * par + 128],
                            Pb[:, slot, par, 128 * kt:128 * kt + 128], ident[:, :])
                if kp == c:
                    self.p_free[slot] = [t]
                x = self.pt_at % 2
                self.pt_at += 1
                AC.wait(t, *self.pt_free[x])
                ta = AC.activation(PT[:, x, 0, :], PS[:, self.TB, :], ACT.Copy)
                DV.wait(ta)
                tl = DV.tensor_tensor(PT[:, x, 1, :], PS[:, self.TB, :], PT[:, x, 0, :].bitcast(F), ALU.subtract)
                bank_free[self.TB] = [ta, tl]
                if pending is not None:
                    pv(*pending)
                pending = (kp, (x, ta, tl))
                yield
            t = pv(*pending)
            qc = slice(256 * c, 256 * c + 256)
            if u.kind == DIFF:
                DV.wait(t, *self.mix_free)
                t = DV.tensor_copy(mix[:, qc], PS[:, self.OB, 0:256])
                bank_free[self.OB] = [t]
            else:
                i, st = next_stage(AC)
                AC.wait(t)
                ta = AC.activation(st[0:64, 0:256], PS[64:128, self.OB, 0:256], ACT.Copy)
                DV.wait(ta, *self.mix_free)
                t = DV.tensor_tensor(mix[64 * a:64 * a + 64, qc], PS[0:64, self.OB, 0:256], st[0:64, 0:256], ALU.add)
                bank_free[self.OB] = [ta, t]
                stage_free[i] = [t]
            if c < 3 or (u.kind != DIFF and a == 0):
                return
            row = u.index + (0 if u.kind == DIFF else 4)
            if u.kind == DIFF:
                yield
                for half in range(2):
                    cc = slice(512 * half, 512 * half + 512)
                    i, sq = next_stage(AC)
                    AC.wait(t)
                    ts = AC.activation(sq, mix[:, cc], ACT.Square)
                    b = self.OB
                    claim(b)
                    PE.wait(ts, t_ones)
                    tp = PE.matmul(PS[:, b, :], ones[:, :], sq, start=True, stop=True)
                    stage_free[i] = [tp]
                    yield
                    i, va = next_stage(DV)
                    j, y = next_stage(AC)
                    l, w = next_stage(AC)
                    DV.wait(tp)
                    tv = DV.tensor_scalar(va, PS[:, b, :], 1.0 / 128, EPS1, ALU.mult, ALU.add)
                    bank_free[b] = [tv]
                    AC.wait(tv)
                    AC.activation(y, va, ACT.Ln)
                    AC.after().activation(y, y, ACT.Exp, scale=-0.5)
                    tw = AC.after().activation(w, y, ACT.Square)
                    DV.wait(tw)
                    DV.scalar_tensor_tensor(w, w, -0.5, va, ALU.mult, ALU.mult)
                    DV.after().scalar_tensor_tensor(w, w, 1.5, y, ALU.add, ALU.mult)
                    DV.wait(g08)
                    tn = DV.after().scalar_tensor_tensor(mix[:, cc], mix[:, cc], sm[:, 1:2], w, ALU.mult, ALU.mult)
                    for z in (i, j, l):
                        stage_free[z] = [tn]
                    yield
                t = tn
            td = dma("mix", scr_mix[row], mix[:, :], waits=[t])
            self.mix_free = [td]
            self.spills[row] = td

        def advance(self):
            if self.steps:
                try:
                    next(self.steps[0])
                except StopIteration:
                    self.steps.pop(0)
                    self.advance_free = True

        def unit(self, u, fill, per_slot):
            groups = [(0, c) for c in range(4)] if u.kind == DIFF else [(a, c) for a in range(2) for c in range(4)]
            for a, c in groups:
                while len(self.steps) > 1:
                    self.advance()
                slot = self.group % 2
                todo = [(x, i) for i in (2 * c, 2 * c + 1) for x in ((0, 1) if u.kind == DIFF else (a,))]
                jobs, last = [], None
                for x, i in todo:
                    j = self.scores(u, x, i)
                    self.advance()
                    self.soft1(j)
                    if last is not None:
                        self.soft2(last)
                    if len(self.steps) > 1:
                        self.advance()
                    last = j
                    jobs.append(j)
                    fill(per_slot)
                self.soft2(last)
                self.steps.append(self.group_steps(u, a, c, jobs, slot))
                self.group += 1

        def finish(self, fill, n):
            while self.steps:
                self.advance()
                fill(n)

    zcol = vec[:, NV:NV + 1]
    t_zero = DV.memset(vec[:, NV:NV + 3], 0.0)

    def zeros_for(n):
        return zcol.broadcast_to([128, n])

    def filler(gens):
        gens = list(gens)

        def fill(n):
            while n > 0 and gens:
                try:
                    next(gens[0])
                    n -= 1
                except StopIteration:
                    gens.pop(0)
        return fill, gens

    def attend(att, units, names, src, freed, start, after):
        for n, u in enumerate(units):
            gens = []
            if n + 1 < len(units):
                prev = units[n - 1] if n else None
                gens = [project(units[n + 1], names[n + 1][0], names[n + 1][1], src, prev, freed)]
            else:
                gens = after()
            if start.get(n):
                start[n](att)
            fill, left = filler(gens)
            att.unit(u, fill, 3)
            while left:
                fill(1)
        return att

    dense_banks[:] = [6, 7]
    names1 = [("w_in", (u, 4 + u, 8 + u)) for u in range(4)] + [("w_in", (12 + u, 16 + u, 20 + u)) for u in range(4)]
    units1 = [Unit(DIFF, u, RG[1], u % 2) for u in range(4)] + [Unit(FOX, u, RG[1], u % 2) for u in range(4)]
    run(project(units1[0], *names1[0], RG[0], None, []))

    def fox_start(att):
        t1 = dma("tab", TABR[:, 0, :].bitcast(F), scr_ct, waits=[units1[3].rope_done, t_ct])
        t2 = dma("sel", P2[:, 0:S], cst[:, C_SEL:C_SEL + S], waits=att.p2_free + att_last_p2(att))
        AC.wait(t2, units1[3].rope_done)
        t3 = AC.activation(TABR[:, 1, :], P2[:, 0:S], ACT.Copy)
        att.bias = [t1, t3]
        att.p2_free = [t3]
        att.mask = [load_mask(FOX, [units1[3].qk_done])]

    def att_last_p2(att):
        return []

    h_dead1 = [None]

    def mix_load(rows, dst, att, freed, out_ready):
        for r in rows:
            for half in range(2):
                cc = slice(512 * half, 512 * half + 512)
                i, st = next_stage(SP)
                t = dma(f"st{i}", st, scr_mix[r][:, cc], waits=[att.spills[r]])
                AC.wait(t, *freed)
                ta = AC.activation(dst[:, 0, r, cc], st, ACT.Copy)
                DV.wait(ta)
                tl = DV.tensor_tensor(dst[:, 1, r, cc], st, dst[:, 0, r, cc].bitcast(F), ALU.subtract)
                stage_free[i] = [ta, tl]
                out_ready[r] += [ta, tl]
                yield

    mix_ready = [[] for _ in range(8)]
    att1 = Attention([x_dead, t_cq, t_ct], [t_mask], [])

    def after1():
        last_pe = [t for f, t in PE.items if f is not None][-1]
        return [mix_load(range(0, 6), RG[0], att1, [last_pe], mix_ready)]

    last_pe_dense = lambda: [t for f, t in PE.items if f is not None][-1]
    attend(att1, units1, names1, RG[0], [], {4: fox_start}, after1)
    att1.finish(lambda n: None, 0)
    run(mix_load(range(6, 8), RG[0], att1, [], mix_ready))

    def post_x(e, g_col, dst, acc, first, g2_col=None, acc2=None):
        tx = post_x.last
        AC.wait(*tx)
        if e == 0:
            AC.wait(*first)
            ts = AC.activation(acc[:, :], XF[:, e, :], ACT.Square)
            post_x.acc = ts
        else:
            AC.wait(post_x.acc)
            ts = AC.activation(P2[:, 0:S], XF[:, e, :], ACT.Square)
            DV.wait(ts, post_x.acc)
            post_x.acc = DV.tensor_tensor(acc[:, :], acc[:, :], P2[:, 0:S], ALU.add)
        if acc2 is not None:
            if e == 0:
                post_x.acc2 = AC.activation(acc2[:, :], XF[:, e, :], ACT.Square, scale=v(g2_col + e))
            else:
                AC.wait(post_x.acc)
                ts = AC.activation(P2[:, 0:S], XF[:, e, :], ACT.Square, scale=v(g2_col + e))
                DV.wait(ts, post_x.acc2)
                post_x.acc = post_x.acc2 = DV.tensor_tensor(acc2[:, :], acc2[:, :], P2[:, 0:S], ALU.add)
        if dst is None:
            return []
        AC.wait(*first)
        ta = AC.activation(dst[:, 0, e, :], XF[:, e, :], ACT.Copy, scale=g_col(e))
        DV.wait(ta)
        tl = DV.scalar_tensor_tensor(dst[:, 1, e, :], XF[:, e, :], g_col(e), dst[:, 0, e, :].bitcast(F), ALU.mult, ALU.subtract)
        return [ta, tl]

    def out_projection(name, src, src_ready, xsrc, xwait, dst, g_col, freed):
        ready = [[] for _ in range(8)]
        for e in range(8):
            done = []

            def evac(half, b, t, e=e, done=done):
                cc = slice(512 * half, 512 * half + 512)
                i, st = next_stage(SP)
                tx = dma(f"st{i}", st, xsrc[e][:, cc], waits=xwait)
                DV.wait(t, tx, *freed)
                td = DV.tensor_tensor(XF[:, e, cc], PS[:, b, :], st, ALU.add)
                bank_free[b] = [td]
                stage_free[i] = [td]
                done.append(td)

            run(dense(name, e, 0, 8, src, evac, src_ready if e == 0 else None))
            post_x.last = done
            ready[e] = post_x(e, g_col, dst, mix, freed)
        return ready

    dense_banks[:] = list(range(8))
    freed = [last_pe_dense()] + att1.mix_free + att1.p2_free
    g2 = lambda e: v(V_G2 + e)
    h_ready = out_projection("w_out", RG[0], mix_ready, args["xT"], [], RG[1], g2, freed)

    def make_rstd(dim, eps, acc_t):
        ts = [rsqrt_of(mix, h, dim, eps, rstd, [acc_t] + rstd_ready) for h in range(2)]
        rstd_ready[:] = ts

    def ffn(groups, up, down, src, src_ready, hid, act, post):
        t0 = 0
        down_done = [last_pe_dense()]
        ready = None
        for gi, n in enumerate(groups):
            hr = [[] for _ in range(n)]
            for i in range(n):
                act(t0 + i, i, src, src_ready if (gi == 0 and i == 0) else None, hid, hr, down_done)
            lastg = gi == len(groups) - 1
            for e in range(8):
                done = []

                def evac(half, b, t, e=e, done=done):
                    cc = slice(512 * half, 512 * half + 512)
                    DV.wait(t)
                    td = DV.tensor_tensor(XF[:, e, cc], PS[:, b, :], XF[:, e, cc], ALU.add)
                    bank_free[b] = [td]
                    done.append(td)

                run(dense(down, e, t0, n, hid, evac, hr if e == 0 else None))
                if lastg:
                    post(e, done)
            down_done = [last_pe_dense()]
            t0 += n

    rs_made = [False]

    def swiglu(t, i, src, src_ready, hid, hr, freed):
        gs = []

        def evac_g(half, b, tk):
            cc = slice(512 * half, 512 * half + 512)
            k, st = next_stage(DV)
            DV.wait(tk, *rstd_ready)
            td = DV.tensor_tensor(st, PS[:, b, :], rstd[:, cc], ALU.mult)
            bank_free[b] = [td]
            AC.wait(td)
            ta = AC.activation(st, st, ACT.Silu)
            gs.append((k, st, ta))

        def evac_u(half, b, tk):
            cc = slice(512 * half, 512 * half + 512)
            g, gst, ta = gs[half]
            k, st = next_stage(DV)
            DV.wait(tk)
            td = DV.tensor_tensor(st, PS[:, b, :], rstd[:, cc], ALU.mult)
            bank_free[b] = [td]
            DV.wait(ta)
            tm = DV.after().tensor_tensor(st, st, gst, ALU.mult)
            stage_free[g] = [tm]
            AC.wait(tm, *freed)
            th = AC.activation(hid[:, 0, i, cc], st, ACT.Copy)
            DV.wait(th)
            tl = DV.tensor_tensor(hid[:, 1, i, cc], st, hid[:, 0, i, cc].bitcast(F), ALU.subtract)
            stage_free[k] = [th, tl]
            hr[i] += [th, tl]

        gen = dense("w_gate", t, 0, 8, src, evac_g, src_ready)
        if t == 0:
            for _ in range(6):
                next(gen)
            make_rstd(S, EPS1, post_x.acc)
        run(gen)
        run(dense("w_up", t, 0, 8, src, evac_u))

    gfa = sm[:, 24:32]
    DV.wait(t_vec)
    t_gfa = DV.tensor_tensor(gfa, vec[:, V_GF:V_GF + 8], vec[:, V_GA:V_GA + 8], ALU.mult)
    ready2 = [[] for _ in range(8)]
    x2_first = []

    def post1(e, done):
        post_x.last = done
        ready2[e] = post_x(e, lambda e: gfa[:, e:e + 1], RG[1], mix, rstd_ready + [t_gfa, up_last(), ] if e == 0 else [], V_GF, rstd)

    def up_last():
        return [t for f, t in DV.items if f is not None][-1]

    ffn([8, 7, 7], ["w_gate", "w_up"], "w_down", RG[1], h_ready, RG[0], swiglu, post1)

    R1, R2_ = mix, rstd
    t_a1, t_a2 = post_x.acc, post_x.acc2
    r1 = TABF_ = P2[:, 0:S]
    tr1 = [rsqrt_of(mix, h, S, EPS1, r1, [t_a1, t_a2]) for h in range(2)]

    def scaled(h):
        def extra(va, ps, cols):
            DV.wait(*tr1)
            DV.tensor_tensor(va, ps, r1[:, cols], ALU.mult)
            return DV.after().tensor_tensor(va, va, r1[:, cols], ALU.mult)
        return extra

    tr2 = [rsqrt_of(rstd, h, S, EPS2, mix, [t_a2, *tr1], extra=scaled(h)) for h in range(2)]
    DV.wait(*tr2)
    t_rs = DV.tensor_tensor(rstd[:, :], mix[:, :], r1, ALU.mult)
    rstd_ready[:] = [t_rs]
    x2_spill = []
    for e in range(8):
        if e == 0:
            DV.wait(*tr1, *ready2[7])
        tx = DV.scalar_tensor_tensor(XF[:, e, :], XF[:, e, :], v(V_GF + e), r1, ALU.mult, ALU.mult)
        x2_spill.append(dma(f"x{e}", scr_x[e], XF[:, e, :], waits=[tx]))
    p2_dead = tx

    c0 = place["R0"] + 32768
    CV = [at(f"CV{i}", [128, 1056], F, c0 + 4224 * i) for i in range(7)]
    w0 = last_pe_dense()
    cv_free = [[w0] for _ in range(7)]
    zero_pad = {}
    conv_stage = {}
    PAD = 32
    DV.wait(w0)
    for i in (0, 1, 4):
        zero_pad[i] = DV.memset(CV[i][:, 0:PAD], 0.0)

    def conv_evac(fn):
        def evac(half, b, t):
            cc = slice(512 * half, 512 * half + 512)
            pc = slice(PAD + 512 * half, PAD + 512 * half + 512)
            DV.wait(t, *rstd_ready)
            fn(half, b, cc, pc)
        return evac

    lin_done = {}

    def ev_linear(dst_i, offset, key):
        def fn(half, b, cc, pc):
            o = PAD if offset else 0
            DV.wait(*cv_free[dst_i])
            t = DV.tensor_tensor(CV[dst_i][:, o + 512 * half:o + 512 * half + 512], PS[:, b, :], rstd[:, cc], ALU.mult)
            bank_free[b] = [t]
            lin_done[key] = t
        return conv_evac(fn)

    def ev_gate(dst_i):
        def fn(half, b, cc, pc):
            k, st = next_stage(DV)
            td = DV.tensor_tensor(st, PS[:, b, :], rstd[:, cc], ALU.mult)
            bank_free[b] = [td]
            AC.wait(td)
            ta = AC.activation(st, st, ACT.Sigmoid)
            DV.wait(ta)
            t = DV.tensor_tensor(CV[dst_i][:, pc], CV[dst_i][:, pc], st, ALU.mult)
            stage_free[k] = [t]
        return conv_evac(fn)

    def ev_times(dst_i, padded):
        def fn(half, b, cc, pc):
            k, st = next_stage(DV)
            DV.tensor_tensor(st, PS[:, b, :], rstd[:, cc], ALU.mult)
            t = DV.after().tensor_tensor(CV[dst_i][:, pc if padded else cc], CV[dst_i][:, pc if padded else cc], st, ALU.mult)
            bank_free[b] = [t]
            stage_free[k] = [t]
        return conv_evac(fn)

    spills2 = {}

    def taps(src, dst, n, col, bias=None, per=4):
        sh = lambda k: CV[src][:, PAD - (n - 1) + k:PAD - (n - 1) + k + S]
        if bias is None:
            DV.after().tensor_scalar(CV[dst][:, 0:S], sh(0), v(col), None, ALU.mult)
        else:
            DV.after().tensor_scalar(CV[dst][:, 0:S], sh(0), v(col), bias, ALU.mult, ALU.add)
        for k in range(1, n):
            DV.after().scalar_tensor_tensor(CV[dst][:, 0:S], sh(k), v(col + k), CV[dst][:, 0:S], ALU.mult, ALU.add)
            if k % per == 0:
                yield

    def conv_layernorm():
        for half in range(2):
            cc = slice(512 * half, 512 * half + 512)
            b = next_bank()
            PE.wait([t for f, t in DV.items if f is not None][-1])
            for c in range(2):
                t = PE.matmul(PS[:, b, :], ones[:, :], CV[2 + c][:, cc], start=(c == 0), stop=(c == 1))
            i, mu = next_stage(DV)
            DV.wait(t)
            t = DV.tensor_scalar(mu, PS[:, b, :], 1.0 / 256, None, ALU.mult)
            bank_free[b] = [t]
            for c in range(2):
                t = DV.after().tensor_tensor(CV[2 + c][:, cc], CV[2 + c][:, cc], mu, ALU.subtract)
            stage_free[i] = [t]
            yield
        AC.wait(t)
        AC.activation(CV[5][:, 0:S], CV[2][:, 0:S], ACT.Square)
        ta = AC.activation(CV[6][:, 0:S], CV[3][:, 0:S], ACT.Square)
        DV.wait(ta)
        ts = DV.tensor_tensor(CV[6][:, 0:S], CV[5][:, 0:S], CV[6][:, 0:S], ALU.add)
        yield
        tn = [rsqrt_of(CV[6], h, 256, LN_EPS, CV[5], [ts]) for h in range(2)]
        yield
        for c in range(2):
            DV.wait(*tn)
            t = DV.after().scalar_tensor_tensor(CV[2 + c][:, 0:S], CV[2 + c][:, 0:S], v(V_LNG + c), CV[5][:, 0:S], ALU.mult, ALU.mult)
            AC.wait(t)
            ta = AC.activation(CV[2 + c][:, 0:S], CV[2 + c][:, 0:S], ACT.Silu, bias=v(V_LNB + c))
            spills2[2 + c] = dma(f"cv{c}", scr_mix[2 + c], CV[2 + c][:, 0:S], waits=[ta])
            yield

    def conv_a(c):
        yield from taps(4, 5, 3, V_CA + 3 * c, per=2)

    def conv_tiles():
        side = []

        def tile(n, evac):
            for _ in dense("w_in2", CONV_TILES[n], 0, 8, RG[1], evac, ready2 if n == 0 else None):
                if side and CNT[0] % 3 == 2:
                    try:
                        next(side[0])
                    except StopIteration:
                        side.pop(0)
                CNT[0] += 1
                yield

        CNT = [0]
        yield from tile(0, ev_linear(0, True, "b0"))
        yield from tile(1, ev_gate(0))
        side.append(taps(0, 2, 31, V_CB, v(V_BCB)))
        yield from tile(2, ev_linear(1, True, "b1"))
        yield from tile(3, ev_gate(1))
        side.append(taps(1, 3, 31, V_CB + 31, v(V_BCB + 1)))
        for c in range(2):
            yield from tile(4 + 3 * c, ev_linear(4, True, "a"))
            yield from tile(5 + 3 * c, ev_times(4, True))
            DV.wait(*cv_free[5])
            for _ in conv_a(c):
                pass
            yield from tile(6 + 3 * c, ev_times(5, False))
            t = [t for f, t in DV.items if f is not None][-1]
            spills2[c] = dma(f"cva{c}", scr_mix[c], CV[5][:, 0:S], waits=[t])
            cv_free[5] = [spills2[c]]
        while side:
            try:
                next(side[0])
                yield
            except StopIteration:
                side.pop(0)
        DV.wait(*cv_free[5])
        AC.wait(*cv_free[5])
        yield from conv_layernorm()

    CONV_TILES[:] = [6, 8, 7, 9, 2, 4, 0, 3, 5, 1]
    run(conv_tiles())

    dense_banks[:] = [6, 7]
    units2 = [Unit(STICK, u, RG[0], u % 2) for u in range(4)]
    names2 = [("w_in2", (10 + u, 14 + u, 18 + u)) for u in range(4)]
    run(project(units2[0], *names2[0], RG[1], None, [w0]))
    t_mask2 = load_mask(STICK, [])
    DV.wait(p2_dead)
    t_w1 = DV.memset(P2[:, S:S + 1], 1.0)
    att2 = Attention([*x2_spill, p2_dead, t_w1, t_rs], [t_mask2], [])
    att2.spills.update(spills2)
    for q in (AC,):
        q.wait(*x2_spill)
    DV.wait(t_zero)
    mix_ready2 = [[] for _ in range(8)]

    def after2():
        last_pe = last_pe_dense()
        return [mix_load(range(0, 6), RG[1], att2, [last_pe], mix_ready2)]

    attend(att2, units2, names2, RG[1], list(spills2.values()), {}, after2)
    att2.finish(lambda n: None, 0)
    run(mix_load(range(6, 8), RG[1], att2, [], mix_ready2))

    dense_banks[:] = list(range(8))
    freed = [last_pe_dense()] + att2.mix_free + att2.p2_free + [x for x in att2.b_used]
    gff = lambda e: v(V_GFF + e)
    h_ready = out_projection("w_out2", RG[1], mix_ready2, scr_x, x2_spill, RG[0], gff, freed)

    def relu2(t, i, src, src_ready, hid, hr, freed):
        def evac(half, b, tk):
            cc = slice(512 * half, 512 * half + 512)
            k, st = next_stage(DV)
            DV.wait(tk, *rstd_ready)
            td = DV.scalar_tensor_tensor(st, PS[:, b, :], 0.0, rstd[:, cc], ALU.max, ALU.mult)
            bank_free[b] = [td]
            AC.wait(td)
            AC.activation(st, st, ACT.Square)
            AC.wait(*freed)
            th = AC.after().activation(hid[:, 0, i, cc], st, ACT.Copy)
            DV.wait(th)
            tl = DV.tensor_tensor(hid[:, 1, i, cc], st, hid[:, 0, i, cc].bitcast(F), ALU.subtract)
            stage_free[k] = [th, tl]
            hr[i] += [th, tl]

        gen = dense("w_ff1", t, 0, 8, src, evac, src_ready)
        if t == 0:
            for _ in range(6):
                next(gen)
            make_rstd(S, EPS2, post_x.acc)
        run(gen)

    def post2(e, done):
        post_x.last = done
        post_x(e, None, None, mix, rstd_ready if e == 0 else [])

    ffn([8, 8, 8, 8], ["w_ff1"], "w_ff2", RG[0], h_ready, RG[1], relu2, post2)
    assert used[0] == len(plan)
    make_rstd(S, EPS2, post_x.acc)
    outs = []
    for half in range(2):
        cc = slice(512 * half, 512 * half + 512)
        for e in range(8):
            DV.wait(rstd_ready[half])
            t = DV.scalar_tensor_tensor(XF[:, e, cc], XF[:, e, cc], v(V_GFIN + e), rstd[:, cc], ALU.mult, ALU.mult)
            outs.append(dma(f"o{e}{half}", out[e][:, cc], XF[:, e, cc], waits=[t]))
    SP.wait(*outs)
    SP.wait(*[rec[2] for rec in dma_sems.values()])

    for q in (PE, DV, AC, SP):
        q.count()
    block = ctx.enter_context(nc.Block())

    @block.sync
    def _(e):
        SP.emit(e)

    @block.tensor
    def _(e):
        PE.emit(e)

    @block.vector
    def _(e):
        DV.emit(e)

    @block.scalar
    def _(e):
        AC.emit(e)


def constants():
    c = np.zeros((128, NC), np.float32)
    c[:, C_ID:C_ID + 128] = np.eye(128)
    inv = (np.float32(500000.0) ** (-np.arange(0, 16, 2, dtype=np.float32) / np.float32(16))).astype(np.float32)
    ang = np.arange(S, dtype=np.float32)[:, None] * inv[None, :]
    cos, sin = np.cos(ang).T, np.sin(ang).T
    c[:, C_COS:C_COS + S] = 1.0
    for o in (0, 64):
        for j in range(8):
            c[o + j + 8, C_PERM + o + j] = 1.0
            c[o + j, C_PERM + o + j + 8] = 1.0
            c[o + j, C_COS:C_COS + S] = cos[j]
            c[o + j + 8, C_COS:C_COS + S] = cos[j]
            c[o + j, C_SIN:C_SIN + S] = -sin[j]
            c[o + j + 8, C_SIN:C_SIN + S] = sin[j]
    for h in range(8):
        for r in (h, 32 + h):
            c[r, C_SEL + 128 * h:C_SEL + 128 * h + 128] = 1.0
    q = np.arange(128)[:, None]
    k = np.arange(256)[None, :]
    for kind in range(3):
        for par in range(2):
            qq = q + 128 * par
            ok = [(k // 64) <= (qq // 64), k <= qq, k < qq][kind]
            o = C_MASK + 512 * kind + 256 * par
            c[:, o:o + 256] = np.where(ok, 0.0, -1e30)
    return c


def kernel(**inputs):
    from contextlib import ExitStack
    import concourse.bacc as _bacc
    from concourse.bass_utils import run_bass_kernel_spmd as _run

    a = {k: np.asarray(x) for k, x in inputs.items()}

    def tiles(w):
        k, e = w.shape
        return np.ascontiguousarray(w.reshape(k // 128, 128, e // 128, 128).transpose(2, 1, 0, 3))

    arrays = {}
    arrays["xT"] = np.ascontiguousarray(a["x"][0].T.reshape(8, 128, S))
    w_in = a["w_in"][0]
    arrays["w_in"] = tiles(w_in[:, 0:3072])
    fg = np.zeros((1024, 128), np.float32)
    vecs = np.zeros((128, NV), np.float32)
    for o in (0, 32, 64, 96):
        fg[:, o:o + 8] = w_in[:, 3072:3080]
        vecs[o:o + 8, V_BF] = a["b_f"][0]
    arrays["w_fg"] = tiles(fg)
    for name, key in (("w_out", "w_out"), ("w_gate", "w_gate"), ("w_up", "w_up"), ("w_down", "w_down"),
                      ("w_in2", "w_in_2"), ("w_out2", "w_out_2"), ("w_ff1", "w_ff1_2"), ("w_ff2", "w_ff2_2")):
        arrays[name] = tiles(a[key][0])
    for col, g in ((V_G1, a["norm1_g"][0]), (V_G2, a["norm2_g"][0]), (V_GF, a["normf_g"]), (V_GA, a["g_attn_2"][0]),
                   (V_GFF, a["g_ffn_2"][0]), (V_GFIN, a["g_final_2"])):
        vecs[:, col:col + 8] = g.reshape(8, 128).T
    vecs[:, V_SUB] = a["subln_g"][0]
    for o in (0, 32):
        vecs[o:o + 8, V_SGN] = -8.0
    for c in range(2):
        cc = slice(128 * c, 128 * c + 128)
        vecs[:, V_CA + 3 * c:V_CA + 3 * c + 3] = a["w_conv_a_2"][0][:, cc].T
        vecs[:, V_CB + 31 * c:V_CB + 31 * c + 31] = a["w_conv_b_2"][0][:, cc].T
        vecs[:, V_BCB + c] = a["b_conv_b_2"][0][cc]
        vecs[:, V_LNG + c] = a["ln_b_g_2"][0][cc]
        vecs[:, V_LNB + c] = a["ln_b_b_2"][0][cc]
    for i, key in enumerate(("lam_q1", "lam_q2", "lam_k1", "lam_k2")):
        vecs[0:64, V_LAM + i] = a[key][0]
    arrays["vecs"] = vecs
    arrays["cst"] = constants()

    nc = _bacc.Bacc("TRN2", target_bir_lowering=False, num_devices=1)
    args = {k: nc.dram_tensor(k + "_dram", x.shape, F, kind="ExternalInput").ap() for k, x in arrays.items()}
    out = nc.dram_tensor("out_0_dram", (8, 128, S), F, kind="ExternalOutput").ap()
    with ExitStack() as ctx:
        program(nc, args, out, ctx)
    r = _run(nc, [{k + "_dram": x for k, x in arrays.items()}], core_ids=[0])
    return np.ascontiguousarray(r.results[0]["out_0_dram"].reshape(1024, S).T)[None]
```

```python
import math

import numpy as np

import concourse.bass as bass
from concourse import mybir

F = mybir.dt.float32
R = mybir.dt.float32r
BF = mybir.dt.bfloat16
ALU = mybir.AluOpType
ACT = mybir.ActivationFunctionType
AX = mybir.AxisListType.X

S = 1024
EPS1 = 1e-5
EPS2 = 1e-6
LN_EPS = 1e-5
LAM_INIT = 0.8 - 0.6 * math.exp(-0.0)

V_G1, V_G2, V_GF, V_GA, V_GFF, V_GFIN = 0, 8, 16, 24, 32, 40
V_SUB, V_BF, V_SGN = 48, 49, 50
V_CA, V_CB, V_BCB, V_LNG, V_LNB, V_LAM = 51, 57, 119, 121, 123, 125
NV = 129
C_ID, C_PERM, C_COS, C_SIN, C_SEL, C_MASK = 0, 128, 256, 1280, 2304, 3328
NC = C_MASK + 3 * 512
DIFF, FOX, STICK = 0, 1, 2


class Token:

    def __init__(self, sem, value=None):
        self.sem, self.value, self.needed = sem, value, False


class Queue:

    def __init__(self, sem):
        self.sem, self.items = sem, []

    def wait(self, *tokens):
        for t in tokens:
            if t is not None:
                t.needed = True
                self.items.append((None, t))

    def do(self, fn):
        t = Token(self.sem)
        self.items.append((fn, t))
        return t

    def after(self):
        self.wait([t for f, t in self.items if f is not None][-1])
        return self

    def matmul(self, *a, **k):
        return self.do(lambda e: e.matmul(*a, **k))

    def transpose(self, *a, **k):
        return self.do(lambda e: e.transpose(*a, **k))

    def activation(self, *a, **k):
        return self.do(lambda e: e.activation(*a, **k))

    def tensor_tensor(self, *a, **k):
        return self.do(lambda e: e.tensor_tensor(*a, **k))

    def tensor_scalar(self, *a, **k):
        return self.do(lambda e: e.tensor_scalar(*a, **k))

    def scalar_tensor_tensor(self, *a, **k):
        return self.do(lambda e: e.scalar_tensor_tensor(*a, **k))

    def tensor_tensor_scan(self, *a, **k):
        return self.do(lambda e: e.tensor_tensor_scan(*a, **k))

    def tensor_copy(self, *a, **k):
        return self.do(lambda e: e.tensor_copy(*a, **k))

    def reduce_max(self, *a, **k):
        return self.do(lambda e: e.reduce_max(*a, **k))

    def reciprocal(self, *a, **k):
        return self.do(lambda e: e.reciprocal(*a, **k))

    def memset(self, *a, **k):
        return self.do(lambda e: e.memset(*a, **k))

    def count(self):
        n = 0
        for fn, t in self.items:
            if fn is not None and t.needed and t.value is None:
                n += 1
                t.value = n

    def emit(self, eng):
        seen = {}
        for fn, t in self.items:
            if fn is None:
                key = id(t.sem)
                if seen.get(key, 0) < t.value:
                    eng.wait_ge(t.sem, t.value)
                    seen[key] = t.value
            else:
                ins = fn(eng)
                if t.needed and t.sem is self.sem:
                    ins.then_inc(t.sem, 1)


def program(nc, args, out, ctx):
    sem = lambda name: ctx.enter_context(nc.semaphore(name))
    PE, DV, AC, SP, PL = (Queue(sem(n)) for n in ("s_pe", "s_dve", "s_act", "s_sp", "s_pool"))

    base = 16512
    place = {}

    def at(name, shape, dt, offset):
        return nc.alloc_sbuf_tensor_at(name, shape, dt, offset=offset)

    def new(name, shape, dt, size):
        nonlocal base
        off = base
        n = 1
        for d in shape[1:]:
            n *= d
        assert n * (2 if dt == BF else 4) <= size
        base += (size + 31) // 32 * 32
        place[name] = off
        return at(name, shape, dt, off)

    RG = [new(f"R{i}", [128, 2, 8, S], R, 65536) for i in range(2)]
    XF = new("X", [128, 8, S], F, 32768)
    x0 = place["X"]
    Pb = at("Pb", [128, 2, 2, S], F, x0)
    PT = at("PT", [128, 2, 2, 512], R, x0 + 16384)
    TABF = at("TABF", [128, 2, S], F, x0 + 24576)
    TABR = at("TABR", [128, 2, S], R, x0 + 24576)
    raw = new("raw", [128, 3, 512], F, 6144)
    wh = new("wh", [128, 4, 512], R, 8192)
    wl = new("wl", [128, 4, 512], R, 8192)
    rstd = new("rstd", [128, S], F, 4096)
    P2 = new("P2", [128, 1032], F, 4128)
    mix = new("mix", [128, S], F, 4096)
    stage = new("stage", [128, 5, 512], F, 10240)
    stage_r = at("stage_r", [128, 5, 512], R, place["stage"])
    ident = new("ident", [128, 128], F, 512)
    identb = new("identb", [128, 128], BF, 256)
    ones = new("ones", [128, 128], F, 512)
    perm = new("perm", [128, 128], F, 512)
    maskb = new("maskb", [128, 2, 256], BF, 1024)
    vec = new("vec", [128, NV + 3], F, (NV + 3) * 4)
    cq = new("cq", [128, 64], F, 256)
    sm = new("sm", [128, 32], F, 128)
    assert base <= 229368
    PS = ctx.enter_context(nc.psum_tensor("PS", [128, 8, 512], F))

    scr_mix = nc.dram_tensor("scr_mix", (8, 128, S), F, kind="Internal").ap()
    scr_x = nc.dram_tensor("scr_x", (8, 128, S), F, kind="Internal").ap()
    scr_ct = nc.dram_tensor("scr_ct", (128, S), F, kind="Internal").ap()

    v = lambda i: vec[:, i:i + 1]

    dma_sems = {}

    def dma(slot, dst, src, waits=(), q=None):
        q = q or SP
        if slot not in dma_sems:
            dma_sems[slot] = [sem("d_" + slot), 0, None]
        rec = dma_sems[slot]
        q.wait(*waits)
        if rec[2] is not None:
            q.wait(rec[2])
        rec[1] += 16
        t = Token(rec[0], rec[1])
        rec[2] = t
        q.do(lambda e, s=rec[0]: e.dma_start(dst, src).then_inc(s, 16))
        return t

    bank_free = [[] for _ in range(8)]

    def claim(b):
        PE.wait(*bank_free[b])
        bank_free[b] = []

    dense_banks = [0, 1, 2, 3, 4, 5, 6, 7]
    dense_at = [0]

    def next_bank():
        b = dense_banks[dense_at[0] % len(dense_banks)]
        dense_at[0] += 1
        claim(b)
        return b

    t_banks = []
    t_at = [0]

    def next_t():
        b = t_banks[t_at[0] % len(t_banks)]
        t_at[0] += 1
        claim(b)
        return b

    def side_bank():
        if len(dense_banks) == 1:
            return next_t()
        if len(dense_banks) == 8:
            t_at[0] += 1
            b = (dense_at[0] + 2 + t_at[0] % 4) % 8
            claim(b)
            return b
        b = dense_banks[dense_at[0] % len(dense_banks)]
        claim(b)
        return b

    stage_free = [[] for _ in range(5)]
    stage_at = [0]

    def next_stage(q):
        while stage_free[stage_at[0] % 5] is None:
            stage_at[0] += 1
            assert any(x is not None for x in stage_free)
        i = stage_at[0] % 5
        stage_at[0] += 1
        q.wait(*stage_free[i])
        stage_free[i] = None
        return i, stage[:, i, :]

    t_vec = dma("vec", vec[:, 0:NV], args["vecs"])
    cst = args["cst"]
    t_id = dma("c0", ident[:, :], cst[:, C_ID:C_ID + 128])
    t_pm = dma("c1", perm[:, :], cst[:, C_PERM:C_PERM + 128])
    DV.wait(t_id)
    t_idb = DV.tensor_copy(identb[:, :], ident[:, :])
    t_ones = DV.memset(ones[:, :], 1.0)

    def fetch_mask(kind):
        i, st = next_stage(SP)
        return i, st, dma(f"st{i}", st, cst[:, C_MASK + 512 * kind:C_MASK + 512 * kind + 512])

    def load_mask(fetched, waits):
        i, st, t = fetched
        DV.wait(t, *waits)
        t = DV.tensor_copy(maskb[:, :, :].rearrange("p a b -> p (a b)"), st)
        stage_free[i] = [t]
        return t

    plan = []
    pieces = []
    raw_free = [None] * 3
    hl_free = [None] * 4
    n_load = [0]
    n_split = [0]

    def plan_tile(name, e, k0, nk):
        for k in range(k0, k0 + nk, 4):
            plan.append((name, e, k, min(4, k0 + nk - k)))

    def load_piece():
        n = n_load[0]
        if n >= len(plan) or n >= n_split[0] + 3:
            return
        n_load[0] += 1
        name, e, k, m = plan[n]
        slot = n % 3
        t = dma(f"raw{slot}", raw[:, slot, 0:m * 128].rearrange("p (k c) -> p k c", c=128),
                args[name][e, :, k:k + m, :], waits=[raw_free[slot]])
        pieces.append([t, None, None])

    lo_queue = [PL]

    def split_piece():
        n = n_split[0]
        if n >= len(plan):
            return
        while n_load[0] <= n:
            load_piece()
        n_split[0] += 1
        m = plan[n][3] * 128
        slot, h = n % 3, n % 4
        AC.wait(pieces[n][0], hl_free[h])
        th = AC.activation(wh[:, h, 0:m], raw[:, slot, 0:m], ACT.Copy)
        lo_queue[0].wait(th)
        tl = lo_queue[0].tensor_tensor(wl[:, h, 0:m], raw[:, slot, 0:m], wh[:, h, 0:m].bitcast(F), ALU.subtract)
        raw_free[slot] = tl
        pieces[n][1], pieces[n][2] = th, tl
        while n_load[0] < min(len(plan), n_split[0] + 3):
            load_piece()

    used = [0]

    def dense(name, e, k0, nk, src, evac, src_ready=None, s0=0):
        n_p = (nk + 3) // 4
        first = used[0]
        assert plan[first][:3] == (name, e, k0), (plan[first], name, e, k0)
        used[0] += n_p
        for half in range(2):
            b = next_bank()
            cols = slice(512 * half, 512 * half + 512)
            last = None
            for k in range(nk):
                if half == 0 and k % 4 == 0:
                    while n_split[0] < first + k // 4 + 1:
                        split_piece()
                    PE.wait(pieces[first + k // 4][2])
                if src_ready is not None:
                    PE.wait(*src_ready[s0 + k])
                h = (first + k // 4) % 4
                kc = slice((k % 4) * 128, (k % 4) * 128 + 128)
                sh, sl = src[:, 0, s0 + k, cols], src[:, 1, s0 + k, cols]
                PE.matmul(PS[:, b, :], wh[:, h, kc], sh, start=(k == 0), stop=False)
                PE.matmul(PS[:, b, :], wh[:, h, kc], sl, start=False, stop=False)
                last = PE.matmul(PS[:, b, :], wl[:, h, kc], sh, start=False, stop=(k == nk - 1))
                if half == 1 and (k % 4 == 3 or k == nk - 1):
                    hl_free[(first + k // 4) % 4] = last
                    if n_split[0] < min(len(plan), used[0] + 2 if k == nk - 1 else used[0] + 1):
                        split_piece()
                elif half == 0 and k == nk - 1 and n_split[0] < used[0] + 1:
                    split_piece()
                if k < nk - 1:
                    yield
            evac(half, b, last)
            yield

    def run(gen):
        for _ in gen:
            pass

    def rsqrt_of(acc, dim, eps, dst, waits, extra=None):
        if len(dense_banks) == 8:
            while n_split[0] < min(len(plan), used[0] + 2):
                split_piece()
        halves2 = []
        for half in range(2):
            cols = slice(512 * half, 512 * half + 512)
            b = side_bank()
            PE.wait(t_ones, *waits)
            tp = PE.matmul(PS[:, b, :], ones[:, :], acc[:, cols], start=True, stop=True)
            i, va = next_stage(DV)
            j, y = next_stage(AC)
            DV.wait(tp)
            if extra is None:
                t = DV.tensor_scalar(va, PS[:, b, :], -0.5 / dim, -0.5 * eps, ALU.mult, ALU.add)
                bank_free[b] = [t]
            else:
                t = extra(va, PS[:, b, :], cols)
                bank_free[b] = [t]
                t = DV.after().tensor_scalar(va, va, -0.5 / dim, -0.5 * eps, ALU.mult, ALU.add)
            AC.wait(t)
            AC.activation(y, va, ACT.Ln, scale=-2.0)
            halves2.append((cols, i, va, j, y))
        ty = [AC.after().activation(y, y, ACT.Exp, scale=-0.5) for _, _, _, _, y in halves2]
        done = []
        for (cols, i, va, j, y), t in zip(halves2, ty):
            DV.wait(t)
            DV.tensor_tensor(va, va, y, ALU.mult)
            DV.after().tensor_tensor(va, va, y, ALU.mult)
            t = DV.after().scalar_tensor_tensor(dst[:, cols], va, 1.5, y, ALU.add, ALU.mult)
            stage_free[i] = [t]
            stage_free[j] = [t]
            done.append(t)
        return done

    plan_tile("w_fg", 0, 0, 8)
    for u in range(4):
        for c in (u, 4 + u, 8 + u):
            plan_tile("w_in", c, 0, 8)
    for u in range(4):
        for c in (12 + u, 16 + u, 20 + u):
            plan_tile("w_in", c, 0, 8)
    for k0, nk in ((0, 7), (7, 1)):
        for e in range(8):
            plan_tile("w_out", e, k0, nk)

    def ffn_plan(groups, up, down):
        t = 0
        for n in groups:
            for i in range(t, t + n):
                for w in up:
                    plan_tile(w, i, 0, 8)
            for e in range(8):
                plan_tile(down, e, t, n)
            t += n

    ffn_plan([8, 7, 7], ["w_gate", "w_up"], "w_down")
    CONV_TILES = [6, 8, 7, 9, 2, 4, 0, 3, 5, 1]
    for c in CONV_TILES:
        plan_tile("w_in2", c, 0, 8)
    for u in range(4):
        for c in (10 + u, 14 + u, 18 + u):
            plan_tile("w_in2", c, 0, 8)
    for k0, nk in ((0, 7), (7, 1)):
        for e in range(8):
            plan_tile("w_out2", e, k0, nk)
    ffn_plan([8, 8, 8, 8], ["w_ff1"], "w_ff2")

    hsrc = RG[0]
    ready = [[] for _ in range(8)]
    acc = mix
    tx_all = []
    for e in range(8):
        tx_all.append(dma(f"x{e}", XF[:, e, :], args["xT"][e]))
        if e < 3:
            load_piece()
    t_mask = load_mask(fetch_mask(DIFF), [])
    for _ in range(2):
        split_piece()
    squares = at("SQ", [128, 8, S], F, place["R1"])

    lamc = sm[:, 0:1]
    DV.wait(t_vec)
    DV.tensor_tensor(sm[:, 2:4], vec[:, V_LAM:V_LAM + 2], vec[:, V_LAM + 2:V_LAM + 4], ALU.mult)
    g08 = DV.tensor_scalar(sm[:, 1:2], v(V_SUB), 1.0 - LAM_INIT, None, ALU.mult)
    b = side_bank()
    PE.wait(g08)
    t = PE.matmul(PS[:, b, 0:2], ones[:, :], sm[:, 2:4], start=True, stop=True)
    AC.wait(t)
    t = AC.activation(sm[:, 4:6], PS[:, b, 0:2], ACT.Exp)
    bank_free[b] = [t]
    DV.wait(t)
    DV.tensor_tensor(sm[:, 6:7], sm[:, 5:6], sm[:, 4:5], ALU.subtract)
    t_lam = DV.after().tensor_scalar(lamc, sm[:, 6:7], -LAM_INIT, None, ALU.add)
    for e in range(8):
        tx = tx_all[e]
        if e == 0:
            AC.wait(tx)
            t_sq = AC.activation(acc[:, :], XF[:, 0, :], ACT.Square)
            t_acc = t_sq
        else:
            AC.wait(tx)
            t_sq = AC.activation(squares[:, e, :], XF[:, e, :], ACT.Square)
        AC.wait(t_vec)
        th = AC.activation(hsrc[:, 0, e, :], XF[:, e, :], ACT.Copy, scale=v(V_G1 + e))
        if e:
            PL.wait(t_sq, t_acc)
            t_acc = PL.tensor_tensor(acc[:, :], acc[:, :], squares[:, e, :], ALU.add)
        DV.wait(th)
        tl = DV.scalar_tensor_tensor(hsrc[:, 1, e, :], XF[:, e, :], v(V_G1 + e), hsrc[:, 0, e, :].bitcast(F), ALU.mult, ALU.subtract)
        ready[e] = [th, tl]
    x_dead = tl
    t_tab = dma("tab", TABF[:, :, :].rearrange("p a b -> p (a b)"), cst[:, C_COS:C_COS + 2 * S], waits=[x_dead])
    rstd_ready = []

    A_ = [Pb[:, i // 2, i % 2, :] for i in range(4)]

    def fg_evac(half, b, t):
        cols = slice(512 * half, 512 * half + 512)
        DV.wait(t, x_dead, *rstd_ready)
        bank_free[b] = [DV.tensor_tensor(A_[0][:, cols], PS[:, b, :], rstd[:, cols], ALU.mult)]

    gen = dense("w_fg", 0, 0, 8, hsrc, fg_evac, ready)
    for _ in range(7):
        next(gen)
    rstd_ready += rsqrt_of(acc, S, EPS1, rstd, [t_acc])
    run(gen)
    AC.wait(*bank_free[(dense_at[0] - 1) % 8])
    AC.activation(A_[1], A_[0], ACT.Abs, bias=v(V_BF))
    AC.after().activation(A_[1], A_[1], ACT.Exp, scale=-1.0)
    t_ln = AC.after().activation(A_[1], A_[1], ACT.Ln, bias=1.0)
    t_min = DV.after().tensor_scalar(A_[2], A_[0], v(V_BF), 0.0, ALU.add, ALU.min)

    def running_sum():
        DV.wait(t_ln, t_min)
        DV.tensor_tensor(A_[2], A_[2], A_[1], ALU.subtract)
        DV.memset(A_[0], 1.0)
        t_cum = DV.after().tensor_tensor_scan(A_[3], A_[0], A_[2], 0.0, ALU.mult, ALU.add)
        DV.after().tensor_scalar(A_[1], A_[3], v(V_SGN), None, ALU.mult)
        ctv = PT[:, 0, :, :].rearrange("p a b -> p (a b)")
        t = DV.after().tensor_copy(ctv, A_[1])
        t = DV.after().tensor_tensor(ctv[32:64, :], A_[1][32:64, :], ctv[32:64, :].bitcast(F), ALU.subtract)
        t_ct = dma("ct", scr_ct, ctv.bitcast(F), waits=[t])
        return t_cum, t_ct

    def cum_by_query():
        for half in range(2):
            b = side_bank()
            PE.wait(t_cum, t_id)
            for i in range(4):
                t = PE.transpose(
                    PS[:, b, 128 * i:128 * i + 128], A_[3][:, 512 * half + 128 * i:512 * half + 128 * i + 128], ident[:, :])
            DV.wait(t)
            t = DV.tensor_copy(
                cq[:, 32 * half:32 * half + 32].rearrange("p (t h) -> p t h", h=8),
                PS[:, b, :].rearrange("p (t c) -> p t c", c=128)[:, :, 0:8])
            bank_free[b] = [t]
        return t

    class Unit:
        def __init__(self, kind, index, region, half):
            self.kind, self.index = kind, index
            r = region[:, :, :, :].rearrange("p a b s -> p (a b s)")[:, 8192 * half:8192 * half + 8192]
            part = lambda i: r[:, 2048 * i:2048 * i + 2048].rearrange("p (a s) -> p a s", a=2)
            self.QQ, self.KH, self.KL = part(0), part(1), part(2)
            self.V = r[:, 6144:8192].rearrange("p (t c) -> p t c", c=256)
            self.q, self.k, self.v = [], [], []
            self.qk_done = self.pv_done = None

    A0, B0 = slice(0, 64), slice(64, 128)

    def halves(dst_a, dst_b, st, hi, cc):
        PL.after().tensor_tensor(dst_a, st[A0, :], hi[A0, 0, cc].bitcast(F), ALU.subtract)
        t = PL.after().tensor_tensor(dst_b, st[B0, :], hi[B0, 1, cc].bitcast(F), ALU.subtract)
        PL.after()
        return t

    def project(u, name, cols, src, prev, freed, src_ready=None):
        later = []
        for which in range(3):

            def split(half, i, st, td, which=which):
                cc = slice(512 * half, 512 * half + 512)
                hi, lo = (u.QQ, u.QQ) if which == 0 else (u.KH, u.KL)
                AC.wait(td, *freed)
                PL.wait(*freed)
                if prev is not None:
                    AC.wait(prev.qk_done)
                    PL.wait(prev.qk_done)
                AC.activation(hi[A0, 0, cc], st[A0, :], ACT.Copy)
                ta = AC.activation(hi[B0, 1, cc], st[B0, :], ACT.Copy)
                PL.wait(ta)
                if which == 0:
                    sr = stage_r[:, i, :]
                    tl = halves(sr[A0, :], sr[B0, :], st, hi, cc)
                    moved = [dma(f"ql0{half}", u.QQ[B0, 0, cc].bitcast(F), sr[A0, :].bitcast(F), waits=[tl]),
                             dma(f"ql1{half}", u.QQ[A0, 1, cc].bitcast(F), sr[B0, :].bitcast(F), waits=[tl])]
                    u.q += [ta, *moved]
                    stage_free[i] = [ta, *moved]
                    return
                else:
                    tl = halves(lo[A0, 0, cc], lo[B0, 1, cc], st, hi, cc)
                    u.k += [dma(f"kh0{half}", u.KH[B0, 0, cc].bitcast(F), u.KH[A0, 0, cc].bitcast(F), waits=[ta]),
                            dma(f"kh1{half}", u.KH[A0, 1, cc].bitcast(F), u.KH[B0, 1, cc].bitcast(F), waits=[ta]),
                            dma(f"kl0{half}", u.KL[B0, 0, cc].bitcast(F), u.KL[A0, 0, cc].bitcast(F), waits=[tl]),
                            dma(f"kl1{half}", u.KL[A0, 1, cc].bitcast(F), u.KL[B0, 1, cc].bitcast(F), waits=[tl]), ta, tl]
                stage_free[i] = [ta, tl]

            def rotate(half, i, st, td, split=split):
                cc = slice(512 * half, 512 * half + 512)
                b = side_bank()
                PE.wait(td, t_pm)
                tp = PE.matmul(PS[:, b, :], perm[:, :], st, start=True, stop=True)
                j, s2 = next_stage(DV)
                PL.wait(t_tab, tp)
                PL.tensor_tensor(st, st, TABF[:, 0, cc], ALU.mult)
                DV.wait(t_tab, tp)
                tq = DV.tensor_tensor(s2, PS[:, b, :], TABF[:, 1, cc], ALU.mult)
                bank_free[b] = [tq]
                PL.after().wait(tq)
                td = PL.tensor_tensor(st, st, s2, ALU.add)
                stage_free[j] = [td]
                u.rope_done = td
                split(half, i, st, td)

            def by_tokens(half, i, st, td):
                b = side_bank()
                PE.wait(td, t_id)
                for n in range(4):
                    tp = PE.transpose(PS[:, b, 128 * n:128 * n + 128], st[:, 128 * n:128 * n + 128], ident[:, :])
                stage_free[i] = [tp]
                tt = slice(4 * half, 4 * half + 4)
                AC.wait(tp, *freed)
                if prev is not None:
                    AC.wait(prev.pv_done)
                if u.kind == DIFF:
                    hi, lo = u.V[:, tt, 0:128], u.V[:, tt, 128:256]
                    ps = PS[:, b, :].rearrange("p (t c) -> p t c", c=128)
                else:
                    vv = u.V[:, tt, :].rearrange("p t (a x c) -> p t a x c", a=2, x=2)
                    hi, lo = vv[:, :, :, 0, :], vv[:, :, :, 1, :]
                    ps = PS[:, b, :].rearrange("p (t a c) -> p t a c", a=2, c=64)
                ta = AC.activation(hi, ps, ACT.Copy)
                DV.wait(ta)
                tl = DV.tensor_tensor(lo, ps, hi.bitcast(F), ALU.subtract)
                bank_free[b] = [ta, tl]
                u.v += [ta, tl]

            after = by_tokens if which == 2 else rotate if u.kind == DIFF else split

            def evac(half, b, t, after=after):
                cc = slice(512 * half, 512 * half + 512)
                i, st = next_stage(DV)
                DV.wait(t, *rstd_ready)
                td = DV.tensor_tensor(st, PS[:, b, :], rstd[:, cc], ALU.mult)
                bank_free[b] = [td]
                later.append([3, after, (half, i, st, td)])

            for _ in dense(name, cols[which], 0, 8, src, evac, src_ready if which == 0 else None):
                yield
                if later:
                    later[0][0] -= 1
                    if later[0][0] <= 0:
                        _, fn, a = later.pop(0)
                        fn(*a)
        for _ in range(2):
            yield
        for _, fn, a in later:
            fn(*a)

    class Attention:
        SB, OB = [0, 2], 5

        def __init__(self, freed, mask, bias):
            self.job = 0
            self.group = 0
            self.steps = []
            self.p_free = [list(freed), list(freed)]
            self.pt_free = [list(freed), list(freed)]
            self.pt_at = 0
            self.tail = None
            self.mix_free = list(freed)
            self.p2_free = list(freed)
            self.b_free = list(freed)
            self.freed = freed
            self.mask, self.bias = mask, bias
            self.spills = {}

        def scores(self, u, a, i):
            c, par = i // 2, i % 2
            n = 256 * (c + 1)
            s = self.SB[self.job % 2]
            claim(s)
            claim(s + 1)
            PE.wait(*u.q, *u.k, *self.mask)
            q = u.QQ[:, a, 128 * i:128 * i + 128]
            S2 = PS[:, s:s + 2, :].rearrange("p a b -> p (a b)")
            for k0 in range(0, n, 512):
                k1 = min(n, k0 + 512)
                PE.matmul(S2[:, k0:k1], q, u.KH[:, a, k0:k1], start=True, stop=False)
                if u.kind == FOX:
                    h = 2 * u.index + a
                    PE.wait(*self.bias)
                    PE.matmul(S2[:, k0:k1], TABR[:, 1, 128 * h:128 * h + 128], TABR[:, 0, k0:k1], start=False, stop=False)
                if k1 == n:
                    PE.matmul(S2[:, n - 256:n], identb[:, :], maskb[:, par, :], start=False, stop=False)
                t = PE.matmul(S2[:, k0:k1], q, u.KL[:, a, k0:k1], start=False, stop=True)
            u.qk_done = t
            job = dict(u=u, a=a, i=i, n=n, s=s, S2=S2, t=t, slot=self.group % 2, no=self.job)
            self.job += 1
            return job

        def row_max(self, j):
            n, u, S2 = j["n"], j["u"], j["S2"]
            o = 8 + 8 * (j["no"] % 2)
            if u.kind == STICK:
                return
            DV.wait(j["t"])
            tm = DV.reduce_max(sm[:, o:o + 1], S2[:, 0:n], AX)
            if u.kind == DIFF:
                t = DV.after().tensor_scalar(sm[:, o + 1:o + 2], sm[:, o:o + 1], -0.125, None, ALU.mult)
            else:
                h = 2 * u.index + j["a"]
                cqh = cq[:, 8 * j["i"] + h:8 * j["i"] + h + 1]
                DV.wait(t_cq)
                DV.after().scalar_tensor_tensor(sm[:, o + 2:o + 3], sm[:, o:o + 1], 0.125, cqh, ALU.mult, ALU.add)
                t = DV.after().tensor_tensor(sm[:, o + 1:o + 2], cqh, sm[:, o + 2:o + 3], ALU.subtract)
            j["m"] = [tm, t]

        def soft1(self, j):
            n, u, S2 = j["n"], j["u"], j["S2"]
            par = j["i"] % 2
            o = 8 + 8 * (j["no"] % 2)
            dst = Pb[:, j["slot"], par, 0:n]
            if u.kind == STICK:
                AC.wait(j["t"], *self.p_free[j["slot"]])
                AC.activation(dst, S2[:, 0:n], ACT.Sigmoid, scale=0.125)
                bt = TABF[:, j["no"] % 2, 0:n]
                if j["no"] >= 2:
                    AC.wait(self.b_used[j["no"] % 2])
                t = AC.activation(bt, S2[:, 0:n], ACT.Sigmoid, scale=-0.125)
                bank_free[j["s"]] = [t]
                bank_free[j["s"] + 1] = [t]
                j["e"] = t
                return
            second = u.kind == DIFF and j["a"] == 1
            if second:
                dst = P2[:, 0:n]
                AC.wait(*self.p2_free)
            else:
                AC.wait(*self.p_free[j["slot"]])
            AC.wait(*j["m"])
            t = AC.activation(dst, S2[:, 0:n], ACT.Exp, bias=sm[:, o + 1:o + 2], scale=0.125, accum_out=sm[:, o + 3:o + 4])
            bank_free[j["s"]] = [t]
            bank_free[j["s"] + 1] = [t]
            j["e"] = t

        b_used = [None, None]
        w_read = None

        def soft2(self, j):
            n, u = j["n"], j["u"]
            par = j["i"] % 2
            o = 8 + 8 * (j["no"] % 2)
            dst = Pb[:, j["slot"], par, 0:n]
            DV.wait(j["e"])
            if u.kind == STICK:
                bt = TABF[:, j["no"] % 2, 0:n]
                w = P2[:, S - n:S]
                DV.wait(self.w_read)
                self.b_used[j["no"] % 2] = DV.tensor_tensor_scan(
                    w[:, ::-1], bt[:, ::-1], zeros_for(n), 1.0, ALU.mult, ALU.add)
                j["p"] = DV.after().tensor_tensor(dst, dst, P2[:, S - n + 1:S + 1], ALU.mult)
                self.w_read = j["p"]
                return
            DV.reciprocal(sm[:, o + 4:o + 5], sm[:, o + 3:o + 4])
            if u.kind == DIFF and j["a"] == 1:
                DV.wait(t_lam)
                DV.after().tensor_scalar(sm[:, o + 5:o + 6], sm[:, o + 4:o + 5], lamc, None, ALU.mult)
                t = DV.after().scalar_tensor_tensor(dst, P2[:, 0:n], sm[:, o + 5:o + 6], dst, ALU.mult, ALU.add)
                self.p2_free = [t]
            else:
                t = DV.after().tensor_scalar(dst, dst, sm[:, o + 4:o + 5], None, ALU.mult)
            j["p"] = t

        held = None
        hook = None
        direct = None

        def group_steps(self, u, a, c, jobs, slot, last):
            pending = None
            o_first = [True]

            def pv(kp, ps):
                if o_first[0]:
                    claim(self.OB)
                    PE.wait(*u.v)
                for kk in range(2):
                    kt = 2 * kp + kk
                    cc = slice(256 * kk, 256 * kk + 256)
                    if u.kind == DIFF:
                        terms = [(u.V[:, kt, 0:128], 0), (u.V[:, kt, 128:256], 0), (u.V[:, kt, 0:128], 1)]
                    else:
                        vt = u.V[:, kt, 128 * a:128 * a + 128]
                        terms = [(vt, 0), (vt, 1)]
                    for n, (lhs, x) in enumerate(terms):
                        st = o_first[0]
                        o_first[0] = False
                        fin = kt == 2 * c + 1 and n == len(terms) - 1
                        PE.wait(ps[1 + x])
                        t = PE.matmul(
                            PS[:, self.OB, 0:256], lhs, PT[:, ps[0], x, cc], start=st, stop=fin)
                self.pt_free[ps[0]] = [t]
                u.pv_done = t
                return t

            for kp in range(c + 1):
                tb = next_t()
                PE.wait(jobs[0]["p"], jobs[-1]["p"], *[x["p"] for x in jobs])
                for kk in range(2):
                    for par in range(2):
                        kt = 2 * kp + kk
                        t = PE.transpose(
                            PS[:, tb, 256 * kk + 128 * par:256 * kk + 128 * par + 128],
                            Pb[:, slot, par, 128 * kt:128 * kt + 128], ident[:, :])
                if kp == c:
                    self.p_free[slot] = [t]
                x = self.pt_at % 2
                self.pt_at += 1
                AC.wait(t, *self.pt_free[x])
                ta = AC.activation(PT[:, x, 0, :], PS[:, tb, :], ACT.Copy)
                DV.wait(ta)
                tl = DV.tensor_tensor(PT[:, x, 1, :], PS[:, tb, :], PT[:, x, 0, :].bitcast(F), ALU.subtract)
                bank_free[tb] = [ta, tl]
                if pending is not None:
                    pv(*pending)
                pending = (kp, (x, ta, tl))
                yield
            t = pv(*pending)
            qc = slice(256 * c, 256 * c + 256)
            if u.kind == DIFF:
                DV.wait(t, *self.mix_free)
                t = DV.tensor_copy(mix[:, qc], PS[:, self.OB, 0:256])
                bank_free[self.OB] = [t]
            else:
                i, st = next_stage(AC)
                AC.wait(t)
                ta = AC.activation(st[0:64, 0:256], PS[64:128, self.OB, 0:256], ACT.Copy)
                DV.wait(ta, *self.mix_free)
                t = DV.tensor_tensor(mix[64 * a:64 * a + 64, qc], PS[0:64, self.OB, 0:256], st[0:64, 0:256], ALU.add)
                bank_free[self.OB] = [ta, t]
                stage_free[i] = [t]
            if not last:
                return
            row = u.index + (0 if u.kind == DIFF else 4)
            if u.kind == DIFF:
                yield
                squares = []
                AC.wait(t)
                for half in range(2):
                    i, sq = next_stage(AC)
                    squares.append((i, sq, AC.activation(sq, mix[:, 512 * half:512 * half + 512], ACT.Square)))
                for half in range(2):
                    cc = slice(512 * half, 512 * half + 512)
                    i, sq, ts = squares[half]
                    yield
                    b = self.OB
                    claim(b)
                    PE.wait(ts, t_ones)
                    tp = PE.matmul(PS[:, b, :], ones[:, :], sq, start=True, stop=True)
                    yield
                    y = sq
                    j, va = next_stage(DV)
                    DV.wait(tp)
                    tv = DV.tensor_scalar(va, PS[:, b, :], -0.5 / 128, -0.5 * EPS1, ALU.mult, ALU.add)
                    bank_free[b] = [tv]
                    AC.wait(tv, tp)
                    AC.activation(y, va, ACT.Ln, scale=-2.0)
                    ty = AC.after().activation(y, y, ACT.Exp, scale=-0.5)
                    PL.wait(ty)
                    PL.tensor_tensor(va, va, y, ALU.mult)
                    PL.after().tensor_tensor(va, va, y, ALU.mult)
                    PL.wait(g08)
                    PL.after().tensor_scalar(va, va, 1.5, sm[:, 1:2], ALU.add, ALU.mult)
                    PL.after().tensor_tensor(va, va, y, ALU.mult)
                    tn = PL.after().tensor_tensor(mix[:, cc], mix[:, cc], va, ALU.mult)
                    for z in (i, j):
                        stage_free[z] = [tn]
                    yield
                t = tn
            if self.direct is None:
                td = dma("mix", scr_mix[row], mix[:, :], waits=[t])
                self.mix_free = [td]
                self.spills[row] = td
                return
            dst, ready, free = self.direct
            self.mix_free = []
            for half in range(2):
                cc = slice(512 * half, 512 * half + 512)
                AC.wait(t, free)
                ta = AC.activation(dst[:, 0, row, cc], mix[:, cc], ACT.Copy)
                DV.wait(ta)
                tl = DV.tensor_tensor(dst[:, 1, row, cc], mix[:, cc], dst[:, 0, row, cc].bitcast(F), ALU.subtract)
                ready[row] += [ta, tl]
                self.mix_free += [ta, tl]
            self.spills[row] = None

        def advance(self):
            if self.steps:
                st = self.steps[0]
                st[1] = max(1, st[1] - 1)
                try:
                    next(st[0])
                except StopIteration:
                    self.steps.pop(0)

        def settle(self):
            if self.held is not None:
                self.soft2(self.held)
                self.held = None

        def unit(self, u, fill, per_slot):
            groups = [(0, c) for c in range(4)] if u.kind == DIFF else [(0, c) for c in range(4)] + [(1, c) for c in (3, 2, 1, 0)]
            for gi, (a, c) in enumerate(groups):
                while len(self.steps) > 1:
                    self.advance()
                slot = self.group % 2
                last = gi == len(groups) - 1
                if last and self.hook:
                    self.hook()
                    self.hook = None
                todo = [(x, i) for i in (2 * c, 2 * c + 1) for x in ((0, 1) if u.kind == DIFF else (a,))]
                jobs = []
                for k, (x, i) in enumerate(todo):
                    j = self.scores(u, x, i)
                    self.settle()
                    self.row_max(j)
                    left = sum(st[1] for st in self.steps)
                    n_adv = -(-left // (len(todo) - k))
                    spare = per_slot if u.kind == DIFF else 2 * n_adv - (k == len(todo) - 1)
                    for z in range(n_adv):
                        f = max(1, spare // (n_adv + 1 - z))
                        fill(f)
                        spare -= f
                        self.advance()
                        if z == 0:
                            self.soft1(j)
                    if n_adv == 0:
                        self.soft1(j)
                    fill(max(0, spare))
                    self.held = j
                    jobs.append(j)
                if u.kind == DIFF:
                    n = c + 2 + (7 if last else 0)
                else:
                    n = c + 2
                self.steps.append([self.group_steps(u, a, c, jobs, slot, last), n])
                self.group += 1

        def finish(self, fill, n):
            self.settle()
            while self.steps:
                self.advance()
                fill(n)

    zcol = vec[:, NV:NV + 1]
    t_zero = DV.memset(vec[:, NV:NV + 3], 0.0)

    def zeros_for(n):
        return zcol.broadcast_to([128, n])

    def filler(gens):
        gens = list(gens)

        def fill(n):
            while n > 0 and gens:
                try:
                    next(gens[0])
                    n -= 1
                except StopIteration:
                    gens.pop(0)
        return fill, gens

    def attend(att, units, names, src, freed, start, after, ready):
        for n, u in enumerate(units):
            gens = []
            dense_banks[:], t_banks[:] = ([6, 7], [4]) if u.kind == DIFF else ([6], [4, 7])
            if n + 1 < len(units):
                prev = units[n - 1] if n else None
                gens = [project(units[n + 1], names[n + 1][0], names[n + 1][1], src, prev, freed)]
            else:
                att.direct = (src, ready, last_pe_dense())
                gens = after()
            if start.get(n):
                start[n](att)
            fill, left = filler(gens)
            att.unit(u, fill, 3)
            if n + 1 == len(units):
                dense_banks[:] = [0, 1, 2, 3, 6]
            while left:
                fill(1)
        return att

    names1 = [("w_in", (u, 4 + u, 8 + u)) for u in range(4)] + [("w_in", (12 + u, 16 + u, 20 + u)) for u in range(4)]
    units1 = [Unit(DIFF, u, RG[1], u % 2) for u in range(4)] + [Unit(FOX, u, RG[1], u % 2) for u in range(4)]
    gen = project(units1[0], *names1[0], RG[0], None, [t_acc])
    for i in range(20):
        next(gen)
        if i == 9:
            t_cum, t_ct = running_sum()
    t_cq = cum_by_query()
    run(gen)
    dense_banks[:] = [6]

    fox_mask = []

    def rows_in(att):
        t1 = dma("tab", TABR[:, 0, :].bitcast(F), scr_ct, waits=[units1[3].rope_done, t_ct])
        ts = dma("sel", TABF[:, 1, :], cst[:, C_SEL:C_SEL + S], waits=[units1[3].rope_done])
        att.bias = [t1]
        att.sel = ts
        att.hook = lambda: fox_mask.append(fetch_mask(FOX))

    def fox_start(att):
        AC.wait(att.sel)
        att.bias.append(AC.activation(TABR[:, 1, :], TABF[:, 1, :], ACT.Copy))
        att.mask = [load_mask(fox_mask.pop(), [units1[3].qk_done])]

    last_pe_dense = lambda: [t for f, t in PE.items if f is not None][-1]

    def fetch_row(r, att):
        got = []
        for half in range(2):
            i, st = next_stage(SP)
            got.append((i, st, dma(f"st{i}", st, scr_mix[r][:, 512 * half:512 * half + 512], waits=[att.spills[r]])))
        return got

    def split_row(r, got, dst, ready, freed):
        for half, (i, st, t) in enumerate(got):
            cc = slice(512 * half, 512 * half + 512)
            AC.wait(t, *freed)
            ta = AC.activation(dst[:, 0, r, cc], st, ACT.Copy)
            DV.wait(ta)
            tl = DV.tensor_tensor(dst[:, 1, r, cc], st, dst[:, 0, r, cc].bitcast(F), ALU.subtract)
            stage_free[i] = [ta, tl]
            ready[r] += [ta, tl]

    def first_pass(name, att, src, ready, xsrc, xwait, XP, before, xp_done):
        freed = [last_pe_dense()]
        xs = []

        def fetch_x(n):
            if n < 16:
                i, st = next_stage(SP)
                xs.append((i, st, dma(f"st{i}", st, xsrc[n // 2][:, 512 * (n % 2):512 * (n % 2) + 512], waits=xwait)))

        for e in range(8):

            def evac(half, b, t, e=e):
                cc = slice(512 * half, 512 * half + 512)
                i, st, tx = xs.pop(0)
                DV.wait(t, tx, before.qk_done, before.pv_done)
                td = DV.tensor_tensor(XP[:, e, cc], PS[:, b, :], st, ALU.add)
                bank_free[b] = [td]
                stage_free[i] = [td]
                xp_done[e].append(td)
                fetch_x(2 * e + half + 1)

            gen = dense(name, e, 0, 7, src, evac, ready if e == 0 else None)
            if e == 0:
                got = fetch_row(0, att)
                for _ in range(2):
                    yield
                split_row(0, got, src, ready, freed)
                got = fetch_row(1, att)
                yield
                for k in range(7):
                    if k < 5:
                        split_row(k + 1, got, src, ready, freed)
                        if k < 4:
                            got = fetch_row(k + 2, att)
                    if k == 6:
                        while 6 not in att.spills:
                            att.advance()
                        fetch_x(0)
                    next(gen)
                    yield
            yield from gen

    mix_ready = [[] for _ in range(8)]
    xp_done = [[] for _ in range(8)]
    att1 = Attention([x_dead, t_cq, t_ct], [t_mask], [])
    XP1 = at("XP1", [128, 8, S], F, place["R1"])
    attend(att1, units1, names1, RG[0], [], {3: rows_in, 4: fox_start},
           lambda: [first_pass("w_out", att1, RG[0], mix_ready, args["xT"], [], XP1, units1[6], xp_done)], mix_ready)
    att1.finish(lambda n: None, 0)

    def post_x(e, g_col, dst, acc, first, g2_col=None, acc2=None, held=None):
        tx = post_x.last
        AC.wait(*tx)
        if dst is not None:
            AC.wait(*first)
            ta = AC.activation(dst[:, 0, e, :], XF[:, e, :], ACT.Copy, scale=g_col(e))
        if e == 0:
            AC.wait(*first)
            ts = AC.activation(acc[:, :], XF[:, e, :], ACT.Square)
            post_x.acc = ts
        else:
            AC.wait(post_x.acc)
            ts = AC.activation(P2[:, 0:S], XF[:, e, :], ACT.Square)
            PL.wait(ts, post_x.acc)
            post_x.acc = PL.tensor_tensor(acc[:, :], acc[:, :], P2[:, 0:S], ALU.add)
        if acc2 is not None:
            if e == 0:
                post_x.acc2 = AC.activation(acc2[:, :], XF[:, e, :], ACT.Square, scale=v(g2_col + e))
            else:
                acc1 = post_x.acc
                AC.wait(post_x.acc)
                ts = AC.activation(P2[:, 0:S], XF[:, e, :], ACT.Square, scale=v(g2_col + e))
                DV.wait(ts, post_x.acc2)
                post_x.acc = post_x.acc2 = DV.tensor_tensor(acc2[:, :], acc2[:, :], P2[:, 0:S], ALU.add)
                post_x.acc1 = acc1
        if dst is None:
            return []

        def rest():
            DV.wait(ta)
            tl = DV.scalar_tensor_tensor(dst[:, 1, e, :], XF[:, e, :], g_col(e), dst[:, 0, e, :].bitcast(F), ALU.mult, ALU.subtract)
            return [ta, tl]

        if held is None:
            return rest()
        held.append((e, rest))
        return []

    def second_pass(name, src, src_ready, XP, xp_done, dst, g_col, freed):
        held = []
        ready = [[] for _ in range(8)]
        for e in range(8):
            done = []

            def evac(half, b, t, e=e, done=done):
                cc = slice(512 * half, 512 * half + 512)
                DV.wait(t, *xp_done[e], *freed)
                td = DV.tensor_tensor(XF[:, e, cc], PS[:, b, :], XP[:, e, cc], ALU.add)
                bank_free[b] = [td]
                done.append(td)

            run(dense(name, e, 7, 1, src, evac, src_ready, 7))
            post_x.last = done
            while held:
                f, rest = held.pop(0)
                ready[f] = rest()
            post_x(e, g_col, dst, mix, freed, held=held)
        for f, rest in held:
            ready[f] = rest()
        return ready

    dense_banks[:] = list(range(8))
    freed = [last_pe_dense()] + att1.mix_free + att1.p2_free
    g2 = lambda e: v(V_G2 + e)
    h_ready = second_pass("w_out", RG[0], mix_ready, XP1, xp_done, RG[1], g2, freed)

    def make_rstd(dim, eps, acc_t):
        ts = rsqrt_of(mix, dim, eps, rstd, [acc_t] + rstd_ready)
        rstd_ready[:] = ts

    def ffn(groups, up, down, src, src_ready, hid, act, post):
        t0 = 0
        down_done = [last_pe_dense()]
        ready = None
        for gi, n in enumerate(groups):
            hr = [[] for _ in range(n)]
            for i in range(n):
                act(t0 + i, i, src, src_ready if (gi == 0 and i == 0) else None, hid, hr, down_done)
            lastg = gi == len(groups) - 1
            for e in range(8):
                done = []

                def evac(half, b, t, e=e, done=done):
                    cc = slice(512 * half, 512 * half + 512)
                    DV.wait(t)
                    td = DV.tensor_tensor(XF[:, e, cc], PS[:, b, :], XF[:, e, cc], ALU.add)
                    bank_free[b] = [td]
                    done.append(td)

                run(dense(down, e, t0, n, hid, evac, hr if e == 0 else None))
                if lastg:
                    post(e, done)
            down_done = [last_pe_dense()]
            t0 += n

    rs_made = [False]

    def swiglu(t, i, src, src_ready, hid, hr, freed):
        gs = []

        def evac_g(half, b, tk):
            cc = slice(512 * half, 512 * half + 512)
            k, st = next_stage(DV)
            DV.wait(tk, *rstd_ready)
            td = DV.tensor_tensor(st, PS[:, b, :], rstd[:, cc], ALU.mult)
            bank_free[b] = [td]
            AC.wait(td)
            ta = AC.activation(st, st, ACT.Silu)
            gs.append((k, st, ta))

        def evac_u(half, b, tk):
            cc = slice(512 * half, 512 * half + 512)
            g, gst, ta = gs[half]
            k, st = next_stage(DV)
            DV.wait(tk)
            td = DV.tensor_tensor(st, PS[:, b, :], rstd[:, cc], ALU.mult)
            bank_free[b] = [td]
            DV.wait(ta)
            tm = DV.after().tensor_tensor(st, st, gst, ALU.mult)
            stage_free[g] = [tm]
            AC.wait(tm, *freed)
            th = AC.activation(hid[:, 0, i, cc], st, ACT.Copy)
            DV.wait(th)
            tl = DV.tensor_tensor(hid[:, 1, i, cc], st, hid[:, 0, i, cc].bitcast(F), ALU.subtract)
            stage_free[k] = [th, tl]
            hr[i] += [th, tl]

        gen = dense("w_gate", t, 0, 8, src, evac_g, src_ready)
        if t == 0:
            for _ in range(6):
                next(gen)
            make_rstd(S, EPS1, post_x.acc)
        run(gen)
        run(dense("w_up", t, 0, 8, src, evac_u))

    gfa = sm[:, 24:32]
    DV.wait(t_vec)
    t_gfa = DV.tensor_tensor(gfa, vec[:, V_GF:V_GF + 8], vec[:, V_GA:V_GA + 8], ALU.mult)
    ready2 = [[] for _ in range(8)]
    x2_first = []

    def post1(e, done):
        post_x.last = done
        ready2[e] = post_x(e, lambda e: gfa[:, e:e + 1], RG[1], mix, rstd_ready + [t_gfa, up_last(), ] if e == 0 else [], V_GF, rstd)

    def up_last():
        return [t for f, t in DV.items if f is not None][-1]

    ffn([8, 7, 7], ["w_gate", "w_up"], "w_down", RG[1], h_ready, RG[0], swiglu, post1)

    t_a1, t_a2 = post_x.acc1, post_x.acc2
    r1 = P2[:, 0:S]
    x2_spill = []

    def second_norm():
        tr1 = rsqrt_of(mix, S, EPS1, r1, [t_a1, t_a2])

        def extra(va, ps, cols):
            DV.wait(*tr1)
            DV.tensor_tensor(va, ps, r1[:, cols], ALU.mult)
            return DV.after().tensor_tensor(va, va, r1[:, cols], ALU.mult)

        tr2 = rsqrt_of(rstd, S, EPS2, mix, [t_a2], extra=extra)
        DV.wait(*tr2)
        rstd_ready[:] = [DV.tensor_tensor(rstd[:, :], mix[:, :], r1, ALU.mult)]
        return tr1

    def spill_x(e, tr1):
        DV.wait(*tr1, *ready2[7])
        tx = DV.scalar_tensor_tensor(XF[:, e, :], XF[:, e, :], v(V_GF + e), r1, ALU.mult, ALU.mult)
        x2_spill.append(dma(f"x{e}", scr_x[e], XF[:, e, :], waits=[tx]))
        return tx

    c0 = place["R0"] + 32768
    CV = [at(f"CV{i}", [128, 1056], F, c0 + 4224 * i) for i in range(7)]
    w0 = last_pe_dense()
    cv_free = [[w0] for _ in range(7)]
    zero_pad = {}
    conv_stage = {}
    PAD = 32
    DV.wait(w0)
    for i in (0, 1, 4):
        zero_pad[i] = DV.memset(CV[i][:, 0:PAD], 0.0)

    def conv_evac(fn):
        def evac(half, b, t):
            cc = slice(512 * half, 512 * half + 512)
            pc = slice(PAD + 512 * half, PAD + 512 * half + 512)
            DV.wait(t, *rstd_ready)
            fn(half, b, cc, pc)
        return evac

    lin_done = {}

    def ev_linear(dst_i, offset, key):
        def fn(half, b, cc, pc):
            o = PAD if offset else 0
            DV.wait(*cv_free[dst_i])
            t = DV.tensor_tensor(CV[dst_i][:, o + 512 * half:o + 512 * half + 512], PS[:, b, :], rstd[:, cc], ALU.mult)
            bank_free[b] = [t]
            lin_done[key] = t
        return conv_evac(fn)

    def ev_gate(dst_i):
        def fn(half, b, cc, pc):
            k, st = next_stage(DV)
            td = DV.tensor_tensor(st, PS[:, b, :], rstd[:, cc], ALU.mult)
            bank_free[b] = [td]
            AC.wait(td)
            ta = AC.activation(st, st, ACT.Sigmoid)
            DV.wait(ta)
            t = DV.tensor_tensor(CV[dst_i][:, pc], CV[dst_i][:, pc], st, ALU.mult)
            stage_free[k] = [t]
        return conv_evac(fn)

    def ev_times(dst_i, padded):
        def fn(half, b, cc, pc):
            k, st = next_stage(DV)
            DV.tensor_tensor(st, PS[:, b, :], rstd[:, cc], ALU.mult)
            t = DV.after().tensor_tensor(CV[dst_i][:, pc if padded else cc], CV[dst_i][:, pc if padded else cc], st, ALU.mult)
            bank_free[b] = [t]
            stage_free[k] = [t]
        return conv_evac(fn)

    spills2 = {}

    def aux_taps(src, c, ks, col):
        sh = lambda k: CV[src][:, PAD - 30 + k:PAD - 30 + k + S]
        sum_, used_ = XF[:, c, :], [None, None]
        AC.wait([t for f, t in DV.items if f is not None][-1], *x2_spill)
        t = AC.activation(sum_, sh(ks[0]), ACT.Copy, scale=v(col + ks[0]))
        for n, k in enumerate(ks[1:]):
            yield
            tmp = XF[:, 2 + n % 2, :]
            AC.wait(aux_free[n % 2])
            ta = AC.activation(tmp, sh(k), ACT.Copy, scale=v(col + k))
            PL.wait(ta, t)
            t = PL.tensor_tensor(sum_, sum_, tmp, ALU.add)
            aux_free[n % 2] = t
        aux_done[c] = t

    aux_free = [None, None]
    aux_done = {}

    def shared_taps(src, dst, c, col, bias):
        aux = aux_taps(src, c, [k for k in range(31) if k % 3 == 2], col)
        sh = lambda k: CV[src][:, PAD - 30 + k:PAD - 30 + k + S]
        DV.after().tensor_scalar(CV[dst][:, 0:S], sh(0), v(col), bias, ALU.mult, ALU.add)
        n = 0
        for k in range(1, 31):
            if k % 3 == 2:
                continue
            n += 1
            if n % 2 == 1:
                next(aux, None)
            DV.after().scalar_tensor_tensor(CV[dst][:, 0:S], sh(k), v(col + k), CV[dst][:, 0:S], ALU.mult, ALU.add)
            yield
        for _ in aux:
            pass
        DV.wait(aux_done[c])
        DV.after().tensor_tensor(CV[dst][:, 0:S], CV[dst][:, 0:S], XF[:, c, :], ALU.add)

    def taps(src, dst, n, col, bias=None, per=1):
        sh = lambda k: CV[src][:, PAD - (n - 1) + k:PAD - (n - 1) + k + S]
        if bias is None:
            DV.after().tensor_scalar(CV[dst][:, 0:S], sh(0), v(col), None, ALU.mult)
        else:
            DV.after().tensor_scalar(CV[dst][:, 0:S], sh(0), v(col), bias, ALU.mult, ALU.add)
        for k in range(1, n):
            DV.after().scalar_tensor_tensor(CV[dst][:, 0:S], sh(k), v(col + k), CV[dst][:, 0:S], ALU.mult, ALU.add)
            if k % per == 0:
                yield

    def conv_layernorm():
        for half in range(2):
            cc = slice(512 * half, 512 * half + 512)
            b = next_bank()
            PE.wait([t for f, t in DV.items if f is not None][-1])
            for c in range(2):
                t = PE.matmul(PS[:, b, :], ones[:, :], CV[2 + c][:, cc], start=(c == 0), stop=(c == 1))
            i, mu = next_stage(DV)
            DV.wait(t)
            t = DV.tensor_scalar(mu, PS[:, b, :], 1.0 / 256, None, ALU.mult)
            bank_free[b] = [t]
            for c in range(2):
                t = DV.after().tensor_tensor(CV[2 + c][:, cc], CV[2 + c][:, cc], mu, ALU.subtract)
            stage_free[i] = [t]
            yield
        AC.wait(t)
        AC.activation(CV[5][:, 0:S], CV[2][:, 0:S], ACT.Square)
        ta = AC.activation(CV[6][:, 0:S], CV[3][:, 0:S], ACT.Square)
        DV.wait(ta)
        ts = DV.tensor_tensor(CV[6][:, 0:S], CV[5][:, 0:S], CV[6][:, 0:S], ALU.add)
        yield
        tn = rsqrt_of(CV[6], 256, LN_EPS, CV[5], [ts])
        yield
        for c in range(2):
            DV.wait(*tn)
            t = DV.after().scalar_tensor_tensor(CV[2 + c][:, 0:S], CV[2 + c][:, 0:S], v(V_LNG + c), CV[5][:, 0:S], ALU.mult, ALU.mult)
            AC.wait(t)
            ta = AC.activation(CV[2 + c][:, 0:S], CV[2 + c][:, 0:S], ACT.Silu, bias=v(V_LNB + c))
            spills2[2 + c] = dma(f"cv{c}", scr_mix[2 + c], CV[2 + c][:, 0:S], waits=[ta])
            yield

    def conv_a(c):
        yield from taps(4, 5, 3, V_CA + 3 * c, per=2)

    units2 = [Unit(STICK, u, RG[0], u % 2) for u in range(4)]
    names2 = [("w_in2", (10 + u, 14 + u, 18 + u)) for u in range(4)]

    def conv_tiles():
        side = []
        count = [0]

        def beside(gen):
            for _ in gen:
                count[0] += 1
                if side and count[0] % 2 == 0:
                    try:
                        next(side[0])
                    except StopIteration:
                        side.pop(0)
                yield

        def tile(n, evac):
            yield from beside(dense("w_in2", CONV_TILES[n], 0, 8, RG[1], evac, ready2 if n == 0 else None))

        yield from tile(0, ev_linear(0, True, "b0"))
        yield from tile(1, ev_gate(0))
        side.append(shared_taps(0, 2, 0, V_CB, v(V_BCB)))
        yield from tile(2, ev_linear(1, True, "b1"))
        yield from tile(3, ev_gate(1))
        side.append(shared_taps(1, 3, 1, V_CB + 31, v(V_BCB + 1)))
        for c in range(2):
            yield from tile(4 + 3 * c, ev_linear(4, True, "a"))
            yield from tile(5 + 3 * c, ev_times(4, True))
            DV.wait(*cv_free[5])
            for _ in conv_a(c):
                pass
            yield from tile(6 + 3 * c, ev_times(5, False))
            t = [t for f, t in DV.items if f is not None][-1]
            spills2[c] = dma(f"cva{c}", scr_mix[c], CV[5][:, 0:S], waits=[t])
            cv_free[5] = [spills2[c]]

        def rest():
            DV.wait(*cv_free[5])
            AC.wait(*cv_free[5])
            yield from conv_layernorm()

        side.append(rest())
        yield from beside(project(units2[0], *names2[0], RG[1], None, [w0]))
        while side:
            try:
                next(side[0])
                yield
            except StopIteration:
                side.pop(0)

    gen = conv_tiles()
    for _ in range(7):
        next(gen)
    tr1 = second_norm()
    for e in range(8):
        for _ in range(6):
            next(gen)
        p2_dead = spill_x(e, tr1)
    run(gen)

    dense_banks[:] = [6]
    t_mask2 = load_mask(fetch_mask(STICK), [])
    DV.wait(p2_dead)
    t_w1 = DV.memset(P2[:, S:S + 1], 1.0)
    att2 = Attention([*x2_spill, *aux_done.values(), p2_dead, t_w1, *rstd_ready], [t_mask2], [])
    att2.spills.update(spills2)
    for q in (AC,):
        q.wait(*x2_spill)
    DV.wait(t_zero)
    mix_ready2 = [[] for _ in range(8)]
    xp_done2 = [[] for _ in range(8)]
    XP2 = at("XP2", [128, 8, S], F, place["R0"])
    attend(att2, units2, names2, RG[1], list(spills2.values()), {},
           lambda: [first_pass("w_out2", att2, RG[1], mix_ready2, scr_x, x2_spill, XP2, units2[2], xp_done2)], mix_ready2)
    att2.finish(lambda n: None, 0)

    dense_banks[:] = list(range(8))
    freed = [last_pe_dense()] + att2.mix_free + att2.p2_free + [x for x in att2.b_used]
    gff = lambda e: v(V_GFF + e)
    h_ready = second_pass("w_out2", RG[1], mix_ready2, XP2, xp_done2, RG[0], gff, freed)

    def relu2(t, i, src, src_ready, hid, hr, freed):
        def evac(half, b, tk):
            cc = slice(512 * half, 512 * half + 512)
            k, st = next_stage(DV)
            DV.wait(tk, *rstd_ready)
            td = DV.scalar_tensor_tensor(st, PS[:, b, :], 0.0, rstd[:, cc], ALU.max, ALU.mult)
            bank_free[b] = [td]
            AC.wait(td)
            AC.activation(st, st, ACT.Square)
            AC.wait(*freed)
            th = AC.after().activation(hid[:, 0, i, cc], st, ACT.Copy)
            DV.wait(th)
            tl = DV.tensor_tensor(hid[:, 1, i, cc], st, hid[:, 0, i, cc].bitcast(F), ALU.subtract)
            stage_free[k] = [th, tl]
            hr[i] += [th, tl]

        gen = dense("w_ff1", t, 0, 8, src, evac, src_ready)
        if t == 0:
            for _ in range(6):
                next(gen)
            make_rstd(S, EPS2, post_x.acc)
        run(gen)

    def post2(e, done):
        post_x.last = done
        post_x(e, None, None, mix, rstd_ready if e == 0 else [])

    ffn([8, 8, 8, 8], ["w_ff1"], "w_ff2", RG[0], h_ready, RG[1], relu2, post2)
    assert used[0] == len(plan)
    make_rstd(S, EPS2, post_x.acc)
    outs = []
    for half in range(2):
        cc = slice(512 * half, 512 * half + 512)
        for e in range(8):
            DV.wait(rstd_ready[half])
            t = DV.scalar_tensor_tensor(XF[:, e, cc], XF[:, e, cc], v(V_GFIN + e), rstd[:, cc], ALU.mult, ALU.mult)
            outs.append(dma(f"o{e}{half}", out[e][:, cc], XF[:, e, cc], waits=[t]))
    SP.wait(*outs)
    SP.wait(*[rec[2] for rec in dma_sems.values()])

    for q in (PE, DV, AC, SP, PL):
        q.count()
    block = ctx.enter_context(nc.Block())

    @block.sync
    def _(e):
        SP.emit(e)

    @block.tensor
    def _(e):
        PE.emit(e)

    @block.vector
    def _(e):
        DV.emit(e)

    @block.scalar
    def _(e):
        AC.emit(e)

    @block.gpsimd
    def _(e):
        PL.emit(e)


def constants():
    c = np.zeros((128, NC), np.float32)
    c[:, C_ID:C_ID + 128] = np.eye(128)
    inv = (np.float32(500000.0) ** (-np.arange(0, 16, 2, dtype=np.float32) / np.float32(16))).astype(np.float32)
    ang = np.arange(S, dtype=np.float32)[:, None] * inv[None, :]
    cos, sin = np.cos(ang).T, np.sin(ang).T
    c[:, C_COS:C_COS + S] = 1.0
    for o in (0, 64):
        for j in range(8):
            c[o + j + 8, C_PERM + o + j] = 1.0
            c[o + j, C_PERM + o + j + 8] = 1.0
            c[o + j, C_COS:C_COS + S] = cos[j]
            c[o + j + 8, C_COS:C_COS + S] = cos[j]
            c[o + j, C_SIN:C_SIN + S] = -sin[j]
            c[o + j + 8, C_SIN:C_SIN + S] = sin[j]
    for h in range(8):
        for r in (h, 32 + h):
            c[r, C_SEL + 128 * h:C_SEL + 128 * h + 128] = 1.0
    q = np.arange(128)[:, None]
    k = np.arange(256)[None, :]
    for kind in range(3):
        for par in range(2):
            qq = q + 128 * par
            ok = [(k // 64) <= (qq // 64), k <= qq, k < qq][kind]
            o = C_MASK + 512 * kind + 256 * par
            c[:, o:o + 256] = np.where(ok, 0.0, -1e30)
    return c


def kernel(**inputs):
    from contextlib import ExitStack
    import concourse.bacc as _bacc
    from concourse.bass_utils import run_bass_kernel_spmd as _run

    a = {k: np.asarray(x) for k, x in inputs.items()}

    def tiles(w):
        k, e = w.shape
        return np.ascontiguousarray(w.reshape(k // 128, 128, e // 128, 128).transpose(2, 1, 0, 3))

    arrays = {}
    arrays["xT"] = np.ascontiguousarray(a["x"][0].T.reshape(8, 128, S))
    w_in = a["w_in"][0]
    arrays["w_in"] = tiles(w_in[:, 0:3072])
    fg = np.zeros((1024, 128), np.float32)
    vecs = np.zeros((128, NV), np.float32)
    for o in (0, 32, 64, 96):
        fg[:, o:o + 8] = w_in[:, 3072:3080]
        vecs[o:o + 8, V_BF] = a["b_f"][0]
    arrays["w_fg"] = tiles(fg)
    for name, key in (("w_out", "w_out"), ("w_gate", "w_gate"), ("w_up", "w_up"), ("w_down", "w_down"),
                      ("w_in2", "w_in_2"), ("w_out2", "w_out_2"), ("w_ff1", "w_ff1_2"), ("w_ff2", "w_ff2_2")):
        arrays[name] = tiles(a[key][0])
    for col, g in ((V_G1, a["norm1_g"][0]), (V_G2, a["norm2_g"][0]), (V_GF, a["normf_g"]), (V_GA, a["g_attn_2"][0]),
                   (V_GFF, a["g_ffn_2"][0]), (V_GFIN, a["g_final_2"])):
        vecs[:, col:col + 8] = g.reshape(8, 128).T
    vecs[:, V_SUB] = a["subln_g"][0]
    for o in (0, 32):
        vecs[o:o + 8, V_SGN] = -8.0
    for c in range(2):
        cc = slice(128 * c, 128 * c + 128)
        vecs[:, V_CA + 3 * c:V_CA + 3 * c + 3] = a["w_conv_a_2"][0][:, cc].T
        vecs[:, V_CB + 31 * c:V_CB + 31 * c + 31] = a["w_conv_b_2"][0][:, cc].T
        vecs[:, V_BCB + c] = a["b_conv_b_2"][0][cc]
        vecs[:, V_LNG + c] = a["ln_b_g_2"][0][cc]
        vecs[:, V_LNB + c] = a["ln_b_b_2"][0][cc]
    for i, key in enumerate(("lam_q1", "lam_q2", "lam_k1", "lam_k2")):
        vecs[0:64, V_LAM + i] = a[key][0]
    arrays["vecs"] = vecs
    arrays["cst"] = constants()

    nc = _bacc.Bacc("TRN2", target_bir_lowering=False, num_devices=1)
    args = {k: nc.dram_tensor(k + "_dram", x.shape, F, kind="ExternalInput").ap() for k, x in arrays.items()}
    out = nc.dram_tensor("out_0_dram", (8, 128, S), F, kind="ExternalOutput").ap()
    with ExitStack() as ctx:
        program(nc, args, out, ctx)
    r = _run(nc, [{k + "_dram": x for k, x in arrays.items()}], core_ids=[0])
    return np.ascontiguousarray(r.results[0]["out_0_dram"].reshape(1024, S).T)[None]
```
